# Optimizing a Trainium2 kernel written in Bass

```python
import jax, jax.numpy as jnp
from jax import lax
import numpy as np

D_MODEL = 1024
BATCH = 1
SEQ = 512
DEPTH = 1

HEAD_DIM = 64
FOX_HEADS = 8
SWA_Q_HEADS = 8
SWA_KV_HEADS = 2
SWA_GROUP = SWA_Q_HEADS // SWA_KV_HEADS
WINDOW = 128
Q_BLOCK = 128
D_FF = 2816
ROPE_THETA = 10000.0
RMS_EPS = 1e-6
FOX_WIDTH = FOX_HEADS * HEAD_DIM
SWA_Q_WIDTH = SWA_Q_HEADS * HEAD_DIM
SWA_KV_WIDTH = SWA_KV_HEADS * HEAD_DIM
IN_SPLIT_SIZES = (FOX_WIDTH, FOX_WIDTH, FOX_WIDTH, FOX_HEADS, SWA_Q_WIDTH, SWA_KV_WIDTH, SWA_KV_WIDTH, D_MODEL, D_MODEL)
IN_COLS = sum(IN_SPLIT_SIZES)

kernel_name = "hybrid_fox_swa_sink_macaron"

def rms_norm(x, g):
    xf = x.astype(jnp.float32)
    y = xf * lax.rsqrt(jnp.mean(xf * xf, axis=-1, keepdims=True) + RMS_EPS) * g.astype(jnp.float32)
    return y.astype(x.dtype)

def swiglu(h, w_gate, w_up, w_down):
    return (jax.nn.silu(h @ w_gate) * (h @ w_up)) @ w_down

def rope_tables(seq_len, dtype):
    inv_freq = 1.0 / (ROPE_THETA ** (jnp.arange(0, HEAD_DIM, 2, dtype=jnp.float32) / HEAD_DIM))
    ang = jnp.arange(seq_len, dtype=jnp.float32)[:, None] * inv_freq[None, :]
    return jnp.cos(ang).astype(dtype), jnp.sin(ang).astype(dtype)

def apply_rope(x, cos, sin):
    x1, x2 = jnp.split(x, 2, axis=-1)
    c = cos[None, :, None, :]
    s = sin[None, :, None, :]
    return jnp.concatenate([x1 * c - x2 * s, x2 * c + x1 * s], axis=-1)

def fox_attention(q, k, v, log_f):
    B, S, H, dh = q.shape
    nb = S // Q_BLOCK
    scale = dh ** -0.5
    cum = jnp.cumsum(log_f, axis=1).transpose(0, 2, 1)
    qb = q.reshape(B, nb, Q_BLOCK, H, dh).transpose(1, 0, 2, 3, 4)
    cb = cum.reshape(B, H, nb, Q_BLOCK).transpose(2, 0, 1, 3)
    key_pos = jnp.arange(S)

    def block(args):
        i, q_i, c_i = args
        s = jnp.einsum('bqhd,bkhd->bhqk', q_i, k).astype(jnp.float32) * scale
        s = s + (c_i[..., :, None] - cum[:, :, None, :])
        q_pos = i * Q_BLOCK + jnp.arange(Q_BLOCK)
        causal = key_pos[None, :] <= q_pos[:, None]
        s = jnp.where(causal, s, -jnp.inf)
        p = jax.nn.softmax(s, axis=-1).astype(v.dtype)
        return jnp.einsum('bhqk,bkhd->bqhd', p, v)

    out = lax.map(block, (jnp.arange(nb), qb, cb))
    return out.transpose(1, 0, 2, 3, 4).reshape(B, S, H * dh)

def swa_sink_attention(q, k, v, sinks):
    B, S, Hq, dh = q.shape
    nb = S // WINDOW
    scale = dh ** -0.5
    qb = q.reshape(B, nb, WINDOW, SWA_KV_HEADS, SWA_GROUP, dh)

    def band(t):
        tb = t.reshape(B, nb, WINDOW, SWA_KV_HEADS, dh)
        prev = jnp.pad(tb, ((0, 0), (1, 0), (0, 0), (0, 0), (0, 0)))[:, :-1]
        return jnp.concatenate([prev, tb], axis=2)

    kb, vb = band(k), band(v)
    s = jnp.einsum('bnqhgd,bnkhd->bnhgqk', qb, kb).astype(jnp.float32) * scale
    q_off = jnp.arange(WINDOW)[:, None] + WINDOW
    k_off = jnp.arange(2 * WINDOW)[None, :]
    diff = q_off - k_off
    in_window = (diff >= 0) & (diff < WINDOW)
    exists = (jnp.arange(nb)[:, None] * WINDOW + k_off - WINDOW) >= 0
    mask = in_window[None] & exists[:, None, :]
    s = jnp.where(mask[None, :, None, None], s, -jnp.inf)
    sink = jnp.broadcast_to(sinks.astype(jnp.float32).reshape(1, 1, SWA_KV_HEADS, SWA_GROUP, 1, 1), s.shape[:-1] + (1,))
    p = jax.nn.softmax(jnp.concatenate([s, sink], axis=-1), axis=-1)[..., :-1].astype(v.dtype)
    out = jnp.einsum('bnhgqk,bnkhd->bnqhgd', p, vb)
    return out.reshape(B, S, Hq * dh)

def hybrid_mixer(h, w_in, forget_bias, sinks, w_branch_fox, w_branch_swa, w_out, cos, sin):
    B, S, _ = h.shape
    proj = h @ w_in
    cuts = [int(c) for c in np.cumsum(IN_SPLIT_SIZES)[:-1]]
    q_a, k_a, v_a, f_a, q_b, k_b, v_b, gate_a, gate_b = jnp.split(proj, cuts, axis=-1)
    log_f = jax.nn.log_sigmoid(f_a.astype(jnp.float32) + forget_bias.astype(jnp.float32))
    o_a = fox_attention(q_a.reshape(B, S, FOX_HEADS, HEAD_DIM), k_a.reshape(B, S, FOX_HEADS, HEAD_DIM),
                        v_a.reshape(B, S, FOX_HEADS, HEAD_DIM), log_f)
    qr = apply_rope(q_b.reshape(B, S, SWA_Q_HEADS, HEAD_DIM), cos, sin)
    kr = apply_rope(k_b.reshape(B, S, SWA_KV_HEADS, HEAD_DIM), cos, sin)
    o_b = swa_sink_attention(qr, kr, v_b.reshape(B, S, SWA_KV_HEADS, HEAD_DIM), sinks)
    merged = jax.nn.sigmoid(gate_a) * (o_a @ w_branch_fox) + jax.nn.sigmoid(gate_b) * (o_b @ w_branch_swa)
    return merged @ w_out

def setup_inputs(seed: int = 0) -> dict:
    key = jax.random.key(seed)
    ks = jax.random.split(key, 20)
    f32 = jnp.float32

    def dense(k, fan_in, fan_out):
        return jax.random.normal(k, (DEPTH, fan_in, fan_out), f32) * fan_in ** -0.5

    def gain(k):
        return 1.0 + 0.05 * jax.random.normal(k, (DEPTH, D_MODEL), f32)

    return {
        "x": jax.random.normal(ks[0], (BATCH, SEQ, D_MODEL), f32),
        "ffn1_pre_g": gain(ks[1]),
        "ffn1_post_g": gain(ks[2]),
        "ffn1_w_gate": dense(ks[3], D_MODEL, D_FF),
        "ffn1_w_up": dense(ks[4], D_MODEL, D_FF),
        "ffn1_w_down": dense(ks[5], D_FF, D_MODEL),
        "mix_pre_g": gain(ks[6]),
        "mix_post_g": gain(ks[7]),
        "w_in": dense(ks[8], D_MODEL, IN_COLS),
        "fox_forget_bias": 1.0 + 3.0 * jax.random.uniform(ks[9], (DEPTH, FOX_HEADS), f32),
        "swa_sinks": 0.5 * jax.random.normal(ks[10], (DEPTH, SWA_Q_HEADS), f32),
        "w_branch_fox": dense(ks[11], FOX_WIDTH, D_MODEL),
        "w_branch_swa": dense(ks[12], SWA_Q_WIDTH, D_MODEL),
        "w_out": dense(ks[13], D_MODEL, D_MODEL),
        "ffn2_pre_g": gain(ks[14]),
        "ffn2_post_g": gain(ks[15]),
        "ffn2_w_gate": dense(ks[16], D_MODEL, D_FF),
        "ffn2_w_up": dense(ks[17], D_MODEL, D_FF),
        "ffn2_w_down": dense(ks[18], D_FF, D_MODEL),
    }

def reference(x, ffn1_pre_g, ffn1_post_g, ffn1_w_gate, ffn1_w_up, ffn1_w_down,
              mix_pre_g, mix_post_g, w_in, fox_forget_bias, swa_sinks,
              w_branch_fox, w_branch_swa, w_out,
              ffn2_pre_g, ffn2_post_g, ffn2_w_gate, ffn2_w_up, ffn2_w_down):
    S = x.shape[1]
    cos, sin = rope_tables(S, x.dtype)
    for l in range(DEPTH):
        h = swiglu(rms_norm(x, ffn1_pre_g[l]), ffn1_w_gate[l], ffn1_w_up[l], ffn1_w_down[l])
        x = x + 0.5 * rms_norm(h, ffn1_post_g[l])
        h = hybrid_mixer(rms_norm(x, mix_pre_g[l]), w_in[l], fox_forget_bias[l], swa_sinks[l],
                         w_branch_fox[l], w_branch_swa[l], w_out[l], cos, sin)
        x = x + rms_norm(h, mix_post_g[l])
        h = swiglu(rms_norm(x, ffn2_pre_g[l]), ffn2_w_gate[l], ffn2_w_up[l], ffn2_w_down[l])
        x = x + 0.5 * rms_norm(h, ffn2_post_g[l])
    return x


_drawn_inputs = setup_inputs


def setup_inputs(seed=0):
    import zlib

    import numpy as np

    out = dict(_drawn_inputs(seed))
    spreads = {}
    factors = {'swa_sinks': 8.0, 'ffn2_post_g': 3.62}
    for name, (base, spread) in spreads.items():
        noise = np.random.default_rng([zlib.crc32(name.encode()), seed]).standard_normal(out[name].shape)
        drawn = base * np.exp(spread * noise) if base else spread * noise
        out[name] = __import__('jax').numpy.asarray(drawn.astype(out[name].dtype))
    for name, factor in factors.items():
        out[name] = (out[name] * factor).astype(out[name].dtype)
    return out
```

```python
from contextlib import ExitStack

import numpy as np
import concourse.bass as bass
from concourse import mybir

F32 = mybir.dt.float32
F32R = mybir.dt.float32r
ACT = mybir.ActivationFunctionType
ALU = mybir.AluOpType
AX = mybir.AxisListType

P = 128
D = 1024
S = 512
F = 2816
DH = 64
HEADS = 8
KD = D // P
KF = F // P
TB = S // P
EPS = 1e-6
SCALE = DH ** -0.5
MASKED = -(2.0 ** 126)

RING = 4
UNIT = 8 * P
DOWN_PARTS = (6, 5, 6, 5)
DOWN_FROM = (0, 6, 11, 17)

GATE_UP_UNITS = 2 * KF
DOWN_UNITS = 4 * KD
FFN_UNITS = GATE_UP_UNITS + DOWN_UNITS
Q_A, K_A, FG, V_A, Q_B, K_B, V_B = 0, 4, 8, 9, 13, 17, 18
GATES = 19
OUT = GATES + 3 * KD
MIX_UNITS = OUT + KD
FFN1, MIX, FFN2 = 0, FFN_UNITS, FFN_UNITS + MIX_UNITS

T_QA, T_QB, T_KA, T_KB, T_V, T_PT = 0, 4, 8, 12, 13, 18
T_MERGED = 8


def build(nc, x_in, gu1, dn1, mixw, gu2, dn2, gains, sinks, forget_bias, consts, rope, out):
    with ExitStack() as ctx:
        def sb(name, shape, dt=F32):
            return ctx.enter_context(nc.sbuf_tensor(name, shape, dt))

        def sem(name):
            return ctx.enter_context(nc.semaphore(name))

        xs_hi = sb("xs_hi", [P, KD, S], F32R)
        xs_lo_at = -(-nc.sbuf_base // 32) * 32
        xs_lo = sb("xs_lo", [P, KD, S], F32R)
        h_hi = sb("h_hi", [P, KF, S], F32R)
        h_lo = sb("h_lo", [P, KF, S], F32R)
        w_hi = sb("w_hi", [P, RING, UNIT], F32R)
        w_lo = sb("w_lo", [P, RING, UNIT], F32R)
        ident_r = sb("ident_r", [P, P], F32R)
        mask_r = sb("mask_r", [P, 3, P], F32R)
        pick_r = sb("pick_r", [P, HEADS], F32R)
        cum_r = sb("cum_r", [P, S], F32R)
        x = sb("x", [P, KD, S])
        raw = sb("raw", [P, RING, UNIT])
        tmp = sb("tmp", [P, 4, S])
        sq = sb("sq", [P, 2, S])
        acc_pre = sb("acc_pre", [P, S])
        acc_post = sb("acc_post", [P, S])
        rsb = sb("rsb", [P, S])
        ropes = sb("ropes", [P, 2, S])
        cst = sb("cst", [P, 4 * P + HEADS])
        ones = sb("ones", [P, P])
        gain = sb("gain", [P, 6, KD])
        sink = sb("sink", [P, HEADS])
        nsink = sb("nsink", [P, HEADS])
        fbias = sb("fbias", [HEADS, 1])
        ms = sb("ms", [P, TB])
        rs = sb("rs", [P, TB])
        half = sb("half", [P, TB])
        negmax = sb("negmax", [P, 2, TB])
        rowsum = sb("rowsum", [P, 2, TB])
        sinkexp = sb("sinkexp", [P, 2, TB])
        recip = sb("recip", [P, 2, TB])
        y = nc.alloc_sbuf_tensor_at("y", [P, KD, S], F32, offset=xs_lo_at)
        ps = ctx.enter_context(nc.psum_tensor("ps", [P, 8, S], F32))

        ident = cst[:, 0:P]
        cos, sin = ropes[:, 0, :], ropes[:, 1, :]
        v_hi = h_hi[:, T_V:T_V + 5, :].rearrange("p a b -> p (a b)").rearrange("p (t c) -> p t c", t=TB)
        v_lo = h_lo[:, T_V:T_V + 5, :].rearrange("p a b -> p (a b)").rearrange("p (t c) -> p t c", t=TB)
        pt_hi, pt_lo = h_hi[:, T_PT:T_PT + 4, :], h_lo[:, T_PT:T_PT + 4, :]
        ptb_hi = pt_hi.rearrange("p a b -> p (a b)").rearrange("p (u c) -> p u c", u=2)
        ptb_lo = pt_lo.rearrange("p a b -> p (a b)").rearrange("p (u c) -> p u c", u=2)
        pb = tmp[:, :, :].rearrange("p a b -> p (a b)").rearrange("p (u b c) -> p u b c", u=2, b=TB)

        w_loaded = [sem(f"w_loaded{i}") for i in range(RING)]
        w_hi_made = sem("w_hi_made")
        w_lo_made = sem("w_lo_made")
        w_used = sem("w_used")
        small_loaded = sem("small_loaded")
        gain_loaded = sem("gain_loaded")
        x_loaded = [sem(f"x_loaded{i}") for i in range(KD // 2)]
        fills_made = sem("fills_made")
        consts_split = sem("consts_split")
        pre = [{n: sem(f"pre{i}_{n}") for n in ("hi", "lo", "sq", "acc", "ss", "ms", "rs", "diag", "bc", "rsb")}
               for i in range(3)]
        post = [{n: sem(f"post{i}_{n}") for n in ("sq", "acc", "ss", "ms", "rs", "diag", "bc", "rsb", "t", "x")}
                for i in range(3)]
        ffn = [{n: sem(f"ffn{i}_{n}") for n in ("scaled", "silu", "prod", "hi", "lo", "evac")} for i in range(2)]
        proj_evac = sem("proj_evac")
        proj_val = sem("proj_val")
        proj_hi = sem("proj_hi")
        proj_lo = sem("proj_lo")
        v_hi_made = sem("v_hi_made")
        rope_scaled = sem("rope_scaled")
        rope_parts = sem("rope_parts")
        fgate = sem("fgate")
        fgate_act = sem("fgate_act")
        fox = {n: sem(f"fox_{n}") for n in ("score", "max", "exp", "rec", "norm", "tr", "pth", "ptl", "pv", "oh", "ol")}
        swa = {n: sem(f"swa_{n}") for n in ("score", "rawmax", "max", "exp", "sum", "rec", "norm", "tr", "pth", "ptl",
                                            "pv", "oh")}
        mix_evac = sem("mix_evac")
        gate_scaled = sem("gate_scaled")
        gate_sig = sem("gate_sig")
        branch_parts = sem("branch_parts")
        merged_val = sem("merged_val")
        merged_hi = sem("merged_hi")
        merged_lo = sem("merged_lo")
        stored = sem("stored")

        block = ctx.enter_context(nc.Block())

        def loads_of(u0):
            return u0 % RING, 16 * (u0 // RING + 1)

        @block.sync
        def _(sp):
            def load(u0, i, src, elems):
                if not (isinstance(i, int) and u0 + RING * i < RING):
                    sp.wait_ge(w_lo_made, RING * i + (u0 - RING + 1))
                sp.dma_start(raw[:, u0 % RING, 0:elems], src).then_inc(w_loaded[u0 % RING], 16)

            def ffn_loads(base, gu, dn, first):
                for j in range(RING):
                    if first:
                        sp.dma_start(x[:, 2 * j:2 * j + 2, :], x_in[:, 2 * j:2 * j + 2, :]).then_inc(x_loaded[j], 16)
                    load(base + j, 0, gu[j], UNIT)
                if first:
                    sp.dma_start(cst[:, :], consts).then_inc(small_loaded, 16)
                    sp.dma_start(ropes[:, :, :], rope).then_inc(small_loaded, 16)
                    sp.dma_start(sink[:, :], sinks).then_inc(small_loaded, 16)
                    sp.dma_start(fbias[:, :], forget_bias).then_inc(small_loaded, 16)
                with sp.Fori(1, GATE_UP_UNITS // RING) as i:
                    for j in range(RING):
                        load(base + j, i, gu[bass.ds(RING * i + j, 1)].rearrange("a p n -> (a p) n"), UNIT)
                with sp.Fori(0, KD) as d:
                    for c in range(4):
                        n, at = DOWN_PARTS[c] * P, DOWN_FROM[c] * P
                        load(base + GATE_UP_UNITS + c, d,
                             dn[bass.ds(d, 1), :, at:at + n].rearrange("a p n -> (a p) n"), n)

            sp.dma_start(gain[:, :, :], gains).then_inc(gain_loaded, 16)
            ffn_loads(FFN1, gu1, dn1, True)
            with sp.Fori(0, MIX_UNITS // RING) as i:
                for j in range(RING):
                    load(MIX + j, i, mixw[bass.ds(RING * i + j, 1)].rearrange("a p n -> (a p) n"), UNIT)
            for u in range(MIX_UNITS // RING * RING, MIX_UNITS):
                load(MIX + u, 0, mixw[u], UNIT)
            ffn_loads(FFN2, gu2, dn2, False)
            for k in range(KD):
                sp.wait_ge(post[2]["x"], k + 1)
                sp.dma_start(out[:, k, :], x[:, k, :]).then_inc(stored, 16)
            sp.wait_ge(stored, 16 * KD)

        @block.tensor
        def _(pe):
            def product(o, st, mv, first=False, last=False):
                nc.tensor.matmul(o, st[0], mv[0], start=first, stop=False, skip_group_check=True)
                nc.tensor.matmul(o, st[0], mv[1], start=False, stop=False, skip_group_check=True)
                return nc.tensor.matmul(o, st[1], mv[0], start=False, stop=last, skip_group_check=True)

            def wblock(u0, k, width=P):
                s = u0 % RING
                return w_hi[:, s, k * width:(k + 1) * width], w_lo[:, s, k * width:(k + 1) * width]

            def xtile(k, a=0, b=S):
                return xs_hi[:, k, a:b], xs_lo[:, k, a:b]

            def htile(k, a=0, b=S):
                return h_hi[:, k, a:b], h_lo[:, k, a:b]

            def sum_squares(acc, acc_sem, n, bank, done):
                pe.wait_ge(acc_sem, n)
                for t in range(TB):
                    last = nc.tensor.matmul(ps[:, bank, t:t + 1], acc[:, t * P:(t + 1) * P], ones[:, 0:1],
                                            start=True, stop=True)
                last.then_inc(done, 1)

            def broadcast_factor(n, bank):
                pe.wait_ge(n["diag"], 1)
                nc.tensor.matmul(ps[:, bank, :], ones[:, :], tmp[:, 3, :], start=True, stop=True).then_inc(n["bc"], 1)

            def first_group(base, n):
                pe.wait_ge(w_lo_made, base + 4)
                for k in range(KD // 2):
                    pe.wait_ge(n["lo"], k + 1)
                    for j in range(4):
                        product(ps[:, j, :], wblock(base + j, k), xtile(k), first=(k == 0))
                for j in range(4):
                    for k in range(KD // 2, KD):
                        if j == 0:
                            pe.wait_ge(n["lo"], k + 1)
                        last = product(ps[:, j, :], wblock(base + j, k), xtile(k), last=(k == KD - 1))
                    last.then_inc(w_used, 1)

            def project(u0, i, bank):
                pe.wait_ge(w_lo_made, RING * i + (u0 + 1))
                for k in range(KD):
                    last = product(ps[:, bank, :], wblock(u0, k), xtile(k), first=(k == 0), last=(k == KD - 1))
                last.then_inc(w_used, 1)

            def post_norm(n):
                sum_squares(acc_post, n["acc"], KD + 1, 2, n["ss"])
                broadcast_factor(n, 3)

            def run_ffn(base, f, npre, npost):
                first_group(base, npre)
                sum_squares(acc_pre, npre["acc"], KD + 1, 6, npre["ss"])
                project(base + 4, 0, 4)
                broadcast_factor(npre, 7)
                project(base + 5, 0, 5)

                def tile(t, i):
                    pe.wait_ge(f["evac"], 2 * i + (t - 1))
                    b = 2 * (t % 2)
                    project(base + 2 * t, i, b)
                    project(base + 2 * t + 1, i, b + 1)

                tile(3, 0)
                with pe.Fori(0, (KF - 4) // 2) as i:
                    tile(4, i)
                    tile(5, i)
                with pe.Fori(0, KD // 2) as i:
                    for j in range(2):
                        pe.wait_ge(f["evac"], 2 * i + (KF - 1 + j))
                        for c in range(4):
                            u0 = base + GATE_UP_UNITS + 4 * j + c
                            pe.wait_ge(w_lo_made, 8 * i + (u0 + 1))
                            pe.wait_ge(f["lo"], DOWN_FROM[c] + DOWN_PARTS[c])
                            for k in range(DOWN_PARTS[c]):
                                t = DOWN_FROM[c] + k
                                last = product(ps[:, j, :], wblock(u0, k), htile(t), first=(t == 0), last=(t == KF - 1))
                            last.then_inc(w_used, 1)
                post_norm(npost)

            def fox_scores(h):
                r = DH * (h % 2)
                q, k = T_QA + h // 2, T_KA + h // 2
                for b in range(TB):
                    if h:
                        pe.wait_ge(fox["exp"], 4 * (h - 1) + b + 1)
                    nc.tensor.matmul(ps[:, b, b * P:(b + 1) * P], ident_r[:, :], mask_r[:, 1, :],
                                     start=True, stop=False, skip_group_check=True)
                for b in range(TB):
                    n = (b + 1) * P
                    o = ps[:, b, 0:n]
                    nc.tensor.matmul(o, pick_r[r:r + 40, h:h + 1].to_broadcast([40, P]), cum_r[r:r + 40, 0:n],
                                     start=False, stop=False, skip_group_check=True)
                    product(o, (h_hi[r:r + DH, q, b * P:n], h_lo[r:r + DH, q, b * P:n]),
                            (h_hi[r:r + DH, k, 0:n], h_lo[r:r + DH, k, 0:n]), last=True).then_inc(fox["score"], 1)

            def fox_transpose(h):
                for b in range(TB):
                    pe.wait_ge(fox["norm"], 4 * h + b + 1)
                    if 4 * h + b >= 2:
                        pe.wait_ge(fox["ptl"], 4 * h + b - 1)
                    for j in range(b + 1):
                        last = nc.tensor.transpose(ps[:, 4 + b % 2, j * P:(j + 1) * P], tmp[:, b, j * P:(j + 1) * P],
                                                   ident)
                    last.then_inc(fox["tr"], 1)

            def fox_values(h):
                pe.wait_ge(fox["ptl"], 4 * (h + 1))
                if h >= 2:
                    pe.wait_ge(fox["ol"], h - 1)
                c = P * (h // 2)
                for j in range(TB):
                    last = product(ps[:, 6 + h % 2, j * P:S], (v_hi[:, j, c:c + P], v_lo[:, j, c:c + P]),
                                   (pt_hi[:, j, j * P:S], pt_lo[:, j, j * P:S]), first=(j == 0), last=(j == TB - 1))
                last.then_inc(fox["pv"], 1)

            def swa_scores(h):
                r = DH * (h % 2)
                q = T_QB + h // 2
                if h == 0:
                    pe.wait_ge(fox["exp"], 4 * HEADS)
                elif h >= 2:
                    pe.wait_ge(swa["exp"], h - 1)
                def place(b):
                    return ps[:, 2 * (h % 2) + b // 2, 256 * (b % 2):256 * (b % 2) + 256]

                for b in range(TB):
                    if b == 0:
                        nc.tensor.matmul(place(b)[:, 0:P], ident_r[:, :], mask_r[:, 2, :],
                                         start=True, stop=False, skip_group_check=True)
                        nc.tensor.matmul(place(b)[:, P:2 * P], ident_r[:, :], mask_r[:, 1, :],
                                         start=False, stop=False, skip_group_check=True)
                    else:
                        nc.tensor.matmul(place(b), ident_r[:, :], mask_r[:, 0:2, :].rearrange("p a b -> p (a b)"),
                                         start=(b % 2 == 0), stop=False, skip_group_check=True)
                for b in range(TB):
                    k0, k1 = max(0, b - 1) * P, (b + 1) * P
                    last = product(place(b)[:, 2 * P - (k1 - k0):2 * P],
                                   (h_hi[r:r + DH, q, b * P:k1], h_lo[r:r + DH, q, b * P:k1]),
                                   (h_hi[r:r + DH, T_KB, k0:k1], h_lo[r:r + DH, T_KB, k0:k1]), last=True)
                last.then_inc(swa["score"], 1)

            def swa_transpose(h):
                pe.wait_ge(swa["norm"], h + 1)
                if h == 0:
                    pe.wait_ge(fox["ptl"], 4 * HEADS)
                else:
                    pe.wait_ge(swa["ptl"], 2 * h)
                for j in range(TB):
                    o = ps[:, 4 + j // 2, 256 * (j % 2):256 * (j % 2) + 256]
                    last = nc.tensor.transpose(o[:, 0:P], pb[:, h % 2, j, P:2 * P], ident)
                    if j < TB - 1:
                        last = nc.tensor.transpose(o[:, P:2 * P], pb[:, h % 2, j + 1, 0:P], ident)
                    if j % 2:
                        last.then_inc(swa["tr"], 1)

            def swa_values(h):
                pe.wait_ge(swa["ptl"], 2 * (h + 1))
                if h < 2:
                    pe.wait_ge(fox["ol"], HEADS - 1 + h)
                else:
                    pe.wait_ge(mix_evac, h - 1)
                c = P * (HEADS // 2)
                for j in range(TB):
                    n = min(2 * P, S - j * P)
                    last = product(ps[:, 6 + h % 2, j * P:j * P + n], (v_hi[:, j, c:c + P], v_lo[:, j, c:c + P]),
                                   (ptb_hi[:, h % 2, 256 * j:256 * j + n], ptb_lo[:, h % 2, 256 * j:256 * j + n]),
                                   first=(j == 0), last=(j == TB - 1))
                last.then_inc(swa["pv"], 1)

            def run_mixer():
                npre = pre[1]
                first_group(MIX + Q_A, npre)
                sum_squares(acc_pre, npre["acc"], KD + 1, 6, npre["ss"])
                project(MIX + K_A, 0, 4)
                broadcast_factor(npre, 7)
                project(MIX + K_A + 1, 0, 5)
                for t in (2, 3):
                    pe.wait_ge(proj_evac, t - 1)
                    project(MIX + K_A + t, 0, t - 2)
                project(MIX + FG, 0, 6)
                pe.wait_ge(proj_evac, 6)
                for u in range(4):
                    pe.wait_ge(w_lo_made, MIX + V_A + u + 1)
                    for kk in range(2):
                        k = 2 * u + kk
                        for t in range(TB):
                            last = product(ps[:, 2 + t, :], xtile(k, t * P, (t + 1) * P), wblock(MIX + V_A + u, kk, S),
                                           first=(k == 0), last=(k == KD - 1))
                    last.then_inc(w_used, 1)
                for t, (bank, n) in enumerate(((0, 7), (1, 8), (6, 9), (7, 9))):
                    pe.wait_ge(proj_evac, n)
                    project(MIX + Q_B + t, 0, bank)
                pe.wait_ge(proj_evac, 10)
                project(MIX + K_B, 0, 2)
                pe.wait_ge(proj_evac, 11)
                pe.wait_ge(w_lo_made, MIX + V_B + 1)
                for t in range(TB):
                    for k in range(KD):
                        last = product(ps[:, 3, t * P:(t + 1) * P], xtile(k, t * P, (t + 1) * P),
                                       wblock(MIX + V_B, k), first=(k == 0), last=(k == KD - 1))
                last.then_inc(w_used, 1)

                pe.wait_ge(proj_evac, 19)
                pe.wait_ge(proj_lo, 13)
                pe.wait_ge(fgate, 5)
                pe.wait_ge(consts_split, 1)
                fox_scores(0)
                for h in range(HEADS):
                    fox_transpose(h)
                    if h + 1 < HEADS:
                        fox_scores(h + 1)
                    else:
                        swa_scores(0)
                    fox_values(h)
                for h in range(HEADS):
                    swa_transpose(h)
                    if h + 1 < HEADS:
                        swa_scores(h + 1)
                    swa_values(h)

                with pe.Fori(0, KD // 4) as i:
                    for j in range(4):
                        b = 4 * (j % 2)
                        pe.wait_ge(mix_evac, 4 * i + (HEADS - 1 + j))
                        u0 = MIX + GATES + 3 * j
                        for g in range(2):
                            project(u0 + g, 3 * i, b + g)
                        pe.wait_ge(w_lo_made, 12 * i + (u0 + 3))
                        pe.wait_ge(mix_evac, HEADS)
                        for k in range(4):
                            product(ps[:, b + 2, :], wblock(u0 + 2, k), htile(T_QA + k), first=(k == 0), last=(k == 3))
                        for k in range(4):
                            last = product(ps[:, b + 3, :], wblock(u0 + 2, 4 + k), htile(T_QB + k),
                                           first=(k == 0), last=(k == 3))
                        last.then_inc(w_used, 1)
                with pe.Fori(0, KD // 4) as i:
                    for j in range(4):
                        pe.wait_ge(mix_evac, 4 * i + (HEADS + KD - 1 + j))
                        u0 = MIX + OUT + j
                        pe.wait_ge(w_lo_made, 4 * i + (u0 + 1))
                        pe.wait_ge(merged_lo, KD - 1)
                        for k in range(KD):
                            if k == KD - 1:
                                pe.wait_ge(merged_lo, KD)
                            last = product(ps[:, j % 2, :], wblock(u0, k), htile(T_MERGED + k),
                                           first=(k == 0), last=(k == KD - 1))
                        last.then_inc(w_used, 1)
                post_norm(post[1])

            pe.wait_ge(fills_made, 3)
            run_ffn(FFN1, ffn[0], pre[0], post[0])
            run_mixer()
            run_ffn(FFN2, ffn[1], pre[2], post[2])

        @block.scalar
        def _(act):
            def split_hi(u0, i=0, elems=UNIT):
                s, n = loads_of(u0)
                act.wait_ge(w_loaded[s], 16 * i + n)
                if not (isinstance(i, int) and u0 + RING * i < RING):
                    act.wait_ge(w_used, RING * i + (u0 - RING + 1))
                nc.scalar.activation(w_hi[:, s, 0:elems], raw[:, s, 0:elems], ACT.Copy).then_inc(w_hi_made, 1)

            def copy_factor(n, bank):
                act.wait_ge(n["bc"], 1)
                nc.scalar.activation(rsb[:, :], ps[:, bank, :], ACT.Copy).then_inc(n["rsb"], 1)

            def input_tile(k, n, g):
                nc.scalar.activation(xs_hi[:, k, :], x[:, k, :], ACT.Copy, scale=gain[:, g, k:k + 1]).then_inc(n["hi"], 1)
                if k >= 2:
                    act.wait_ge(n["acc"], k)
                nc.scalar.activation(sq[:, k % 2, :], x[:, k, :], ACT.Square).then_inc(n["sq"], 1)

            def result_tile(d0, i, bank, n, g, used, evac):
                d = i + d0
                act.wait_ge(w_used, used)
                act.wait_ge(n["acc"], d + 1)
                nc.scalar.activation(sq[:, d0 % 2, :], ps[:, bank, :], ACT.Square).then_inc(n["sq"], 1)
                nc.scalar.activation(y[:, bass.ds(d, 1), :].rearrange("p a b -> p (a b)"), ps[:, bank, :], ACT.Copy,
                                     scale=gain[:, g, bass.ds(d, 1)]).then_inc(evac, 1)

            def residual(npost, nnext, g):
                copy_factor(npost, 3)
                if nnext is not None:
                    for k in range(KD):
                        act.wait_ge(npost["x"], k + 1)
                        input_tile(k, nnext, g)

            def run_ffn(base, f, npre, npost, gpost, nnext, gnext, next_base):
                for j in range(4):
                    split_hi(base + 4 + j)
                copy_factor(npre, 7)

                def activate(t, i=0):
                    act.wait_ge(f["scaled"], i + (t + 1))
                    nc.scalar.activation(tmp[:, 0, :], tmp[:, 0, :], ACT.Silu).then_inc(f["silu"], 1)
                    act.wait_ge(f["prod"], i + (t + 1))
                    nc.scalar.activation(h_hi[:, bass.ds(i + t, 1), :].rearrange("p a b -> p (a b)"), tmp[:, 2, :],
                                         ACT.Copy).then_inc(f["hi"], 1)

                activate(0)
                activate(1)

                def tile(t, i):
                    for j in range(2):
                        split_hi(base + 2 * t + 4 + j, i)
                    activate(t, 2 * i)

                with act.Fori(0, (KF - 4) // 2) as i:
                    tile(2, i)
                    tile(3, i)
                for t in (KF - 2, KF - 1):
                    for j in range(2):
                        c = 2 * (t - KF + 2) + j
                        split_hi(base + GATE_UP_UNITS + c, 0, DOWN_PARTS[c] * P)
                    activate(t)

                def down(d0, i, sizes, u0):
                    used = 4 * i + (base + GATE_UP_UNITS + 4 * d0 + 4)
                    for c in range(3):
                        split_hi(u0 + c, i, sizes[c] * P)
                    result_tile(d0, i, d0 % 2, npost, gpost, used, f["evac"])
                    if sizes[3]:
                        split_hi(u0 + 3, i, sizes[3] * P)

                u0 = base + GATE_UP_UNITS + 4
                with act.Fori(0, (KD - 2) // 2) as i:
                    down(0, 2 * i, DOWN_PARTS, u0)
                    down(1, 2 * i, DOWN_PARTS, u0 + 4)
                down(KD - 2, 0, DOWN_PARTS, u0 + 4 * (KD - 2))
                if nnext is not None:
                    down(KD - 1, 0, (8,) * 4, next_base)
                else:
                    result_tile(KD - 1, 0, (KD - 1) % 2, npost, gpost, base + FFN_UNITS, f["evac"])
                residual(npost, nnext, gnext)

            def high_part(n, dst):
                if n < 8:
                    act.wait_ge(proj_evac, n + 1)
                else:
                    act.wait_ge(proj_val, n - 7)
                nc.scalar.activation(dst, tmp[:, 2 + n % 2, :], ACT.Copy).then_inc(proj_hi, 1)

            def fox_exp(h):
                for b in range(TB):
                    act.wait_ge(fox["max"], 4 * h + b + 1)
                    if h:
                        act.wait_ge(fox["tr"], 4 * (h - 1) + b + 1)
                    n = (b + 1) * P
                    nc.scalar.activation(tmp[:, b, 0:n], ps[:, b, 0:n], ACT.Exp, bias=negmax[:, 0, b:b + 1],
                                         accum_out=rowsum[:, 0, b:b + 1]).then_inc(fox["exp"], 1)

            def swa_exp(h):
                p = h % 2
                act.wait_ge(swa["max"], h + 1)
                nc.scalar.activation(sinkexp[:, p, :], negmax[:, p, :], ACT.Exp, bias=sink[:, h:h + 1])
                if h == 0:
                    act.wait_ge(fox["tr"], 4 * HEADS)
                elif h >= 2:
                    act.wait_ge(swa["tr"], 2 * (h - 1))
                for b in range(TB):
                    last = nc.scalar.activation(pb[:, p, b, :],
                                                ps[:, 2 * p + b // 2, 256 * (b % 2):256 * (b % 2) + 256], ACT.Exp,
                                                bias=negmax[:, p, b:b + 1], accum_out=rowsum[:, p, b:b + 1])
                last.then_inc(swa["exp"], 1)

            def run_mixer():
                for j in range(4):
                    split_hi(MIX + 4 + j)
                copy_factor(pre[1], 7)
                for t in range(4):
                    high_part(t, h_hi[:, T_QA + t, :])
                for t in range(4):
                    split_hi(MIX + K_A + t + 4)
                    high_part(4 + t, h_hi[:, T_KA + t, :])
                split_hi(MIX + FG + 4)
                act.wait_ge(fgate, 3)
                nc.scalar.activation(tmp[0:HEADS, 1, :], tmp[0:HEADS, 1, :], ACT.Exp).then_inc(fgate_act, 1)
                act.wait_ge(fgate_act, 1)
                nc.scalar.activation(tmp[0:HEADS, 1, :], tmp[0:HEADS, 1, :], ACT.Ln, bias=1.0).then_inc(fgate_act, 1)
                act.wait_ge(fgate, 4)
                for r in (0, DH):
                    nc.scalar.activation(cum_r[r:r + HEADS, :], tmp[0:HEADS, 0, :], ACT.Copy,
                                         scale=-1.0).then_inc(fgate_act, 1)
                for u in range(4):
                    split_hi(MIX + V_A + u + 4)
                for t in range(TB):
                    nc.scalar.activation(v_hi[:, t, 0:S], ps[:, 2 + t, :], ACT.Copy,
                                         scale=rs[:, t:t + 1]).then_inc(v_hi_made, 1)
                for t in range(4):
                    split_hi(MIX + Q_B + t + 4)
                    high_part(8 + t, h_hi[:, T_QB + t, :])
                split_hi(MIX + K_B + 4)
                high_part(12, h_hi[:, T_KB, :])
                split_hi(MIX + V_B + 4)
                for t in range(TB):
                    nc.scalar.activation(v_hi[:, t, S:S + P], ps[:, 3, t * P:(t + 1) * P], ACT.Copy,
                                         scale=rs[:, t:t + 1]).then_inc(v_hi_made, 1)

                fox_exp(0)
                for h in range(HEADS):
                    for b in range(TB):
                        act.wait_ge(fox["tr"], 4 * h + b + 1)
                        if b == 0 and h:
                            act.wait_ge(fox["pv"], h)
                        nc.scalar.activation(pt_hi[:, 0:b + 1, b * P:(b + 1) * P],
                                             ps[:, 4 + b % 2, 0:(b + 1) * P].rearrange("p (j q) -> p j q", q=P),
                                             ACT.Copy).then_inc(fox["pth"], 1)
                    if h + 1 < HEADS:
                        fox_exp(h + 1)
                    else:
                        swa_exp(0)
                    act.wait_ge(fox["pv"], h + 1)
                    r = DH * (h % 2)
                    nc.scalar.activation(h_hi[r:r + DH, T_QA + h // 2, :], ps[r:r + DH, 6 + h % 2, :],
                                         ACT.Copy).then_inc(fox["oh"], 1)
                for h in range(HEADS):
                    for g, n in ((0, 512), (1, 384)):
                        act.wait_ge(swa["tr"], 2 * h + g + 1)
                        if g == 0 and h >= 2:
                            act.wait_ge(swa["pv"], h - 1)
                        if g == 0 and h < 2:
                            act.wait_ge(fox["pv"], HEADS)
                        nc.scalar.activation(ptb_hi[:, h % 2, 512 * g:512 * g + n], ps[:, 4 + g, 0:n],
                                             ACT.Copy).then_inc(swa["pth"], 1)
                    if h + 1 < HEADS:
                        swa_exp(h + 1)
                    act.wait_ge(swa["pv"], h + 1)
                    r = DH * (h % 2)
                    nc.scalar.activation(h_hi[r:r + DH, T_QB + h // 2, :], ps[r:r + DH, 6 + h % 2, :],
                                         ACT.Copy).then_inc(swa["oh"], 1)

                with act.Fori(0, KD // 4) as i:
                    for j in range(4):
                        u0 = MIX + GATES + 3 * j
                        for g in range(2):
                            split_hi(u0 + 4 + g, 3 * i)
                            act.wait_ge(gate_scaled, 8 * i + (2 * j + g + 1))
                            nc.scalar.activation(tmp[:, g, :], tmp[:, g, :], ACT.Sigmoid).then_inc(gate_sig, 1)
                        split_hi(u0 + 6, 3 * i)
                        act.wait_ge(merged_val, 4 * i + (j + 1))
                        nc.scalar.activation(
                            h_hi[:, bass.ds(4 * i + (T_MERGED + j), 1), :].rearrange("p a b -> p (a b)"),
                            tmp[:, 2, :], ACT.Copy).then_inc(merged_hi, 1)
                with act.Fori(0, KD // 4) as i:
                    for j in range(4):
                        u0 = MIX + OUT + j
                        result_tile(j, 4 * i, j % 2, post[1], 3, 4 * i + (u0 + 1), mix_evac)
                        split_hi(u0 + 4, i)
                residual(post[1], pre[2], 4)

            act.wait_ge(gain_loaded, 16)
            for j in range(KD // 2):
                act.wait_ge(x_loaded[j], 16)
                input_tile(2 * j, pre[0], 0)
                input_tile(2 * j + 1, pre[0], 0)
                split_hi(FFN1 + j)
            act.wait_ge(small_loaded, 64)
            nc.scalar.activation(ident_r[:, :], cst[:, 0:P], ACT.Copy)
            nc.scalar.activation(pick_r[:, :], cst[:, 4 * P:4 * P + HEADS], ACT.Copy)
            nc.scalar.activation(mask_r[:, :, :], cst[:, P:4 * P].rearrange("p (a b) -> p a b", a=3),
                                 ACT.Copy).then_inc(consts_split, 1)
            run_ffn(FFN1, ffn[0], pre[0], post[0], 1, pre[1], 2, MIX)
            run_mixer()
            run_ffn(FFN2, ffn[1], pre[2], post[2], 5, None, None, None)

        @block.vector
        def _(dve):
            def split_lo(u0, i=0, elems=UNIT):
                s = u0 % RING
                dve.wait_ge(w_hi_made, RING * i + (u0 + 1))
                nc.vector.tensor_tensor(w_lo[:, s, 0:elems], raw[:, s, 0:elems], w_hi[:, s, 0:elems].bitcast(F32),
                                        ALU.subtract).then_inc(w_lo_made, 1)

            def low_input(k, n, g):
                dve.wait_ge(n["hi"], k + 1)
                nc.vector.scalar_tensor_tensor(xs_lo[:, k, :], x[:, k, :], gain[:, g, k:k + 1],
                                               xs_hi[:, k, :].bitcast(F32), ALU.mult, ALU.subtract).then_inc(n["lo"], 1)

            def factor(n, bank, c):
                dve.wait_ge(n["ss"], 1)
                nc.vector.tensor_scalar(ms[:, :], ps[:, bank, 0:TB], c ** -2 / D, c ** -2 * EPS,
                                        ALU.mult, ALU.add).then_inc(n["ms"], 1)
                dve.wait_ge(n["rs"], 1)
                nc.vector.tensor_tensor(tmp[:, 3, :].rearrange("p (t q) -> p t q", t=TB),
                                        ident.unsqueeze(1).to_broadcast([P, TB, P]),
                                        rs[:, :].unsqueeze(2).to_broadcast([P, TB, P]), ALU.mult).then_inc(n["diag"], 1)

            def residual(n, nnext, g):
                def scale(k):
                    nc.vector.tensor_tensor(y[:, k, :], y[:, k, :], rsb[:, :], ALU.mult).then_inc(n["t"], 1)

                dve.wait_ge(n["rsb"], 1)
                scale(0)
                for k in range(KD):
                    if k + 1 < KD:
                        scale(k + 1)
                    dve.wait_ge(n["t"], k + 1)
                    nc.vector.tensor_tensor(x[:, k, :], x[:, k, :], y[:, k, :], ALU.add).then_inc(n["x"], 1)
                    if nnext is not None and k:
                        low_input(k - 1, nnext, g)
                if nnext is not None:
                    low_input(KD - 1, nnext, g)

            def run_ffn(base, f, npre, npost, nnext, gnext, next_base):
                nc.vector.memset(acc_post[:, :], 0.0).then_inc(npost["acc"], 1)
                for j in range(4):
                    split_lo(base + 4 + j)
                factor(npre, 6, 1.0)
                dve.wait_ge(npre["rsb"], 1)

                def evacuate(t, i, bank):
                    dve.wait_ge(w_used, 2 * i + (base + 2 * t + 2))
                    nc.vector.tensor_tensor(tmp[:, 0, :], ps[:, bank, :], rsb[:, :], ALU.mult).then_inc(f["scaled"], 1)
                    nc.vector.tensor_tensor(tmp[:, 1, :], ps[:, bank + 1, :], rsb[:, :], ALU.mult).then_inc(f["evac"], 1)
                    dve.wait_ge(f["silu"], i + (t + 1))
                    dve.wait_ge(f["evac"], i + (t + 1))
                    nc.vector.tensor_tensor(tmp[:, 2, :], tmp[:, 0, :], tmp[:, 1, :], ALU.mult).then_inc(f["prod"], 1)
                    dve.wait_ge(f["hi"], i + (t + 1))
                    nc.vector.tensor_tensor(h_lo[:, bass.ds(i + t, 1), :].rearrange("p a b -> p (a b)"), tmp[:, 2, :],
                                            h_hi[:, bass.ds(i + t, 1), :].rearrange("p a b -> p (a b)").bitcast(F32),
                                            ALU.subtract).then_inc(f["lo"], 1)

                evacuate(0, 0, 0)
                evacuate(1, 0, 2)

                def tile(t, i, bank):
                    for j in range(2):
                        split_lo(base + 2 * t + 4 + j, i)
                    evacuate(t, 2 * i, bank)

                tile(2, 0, 4)
                tile(3, 0, 2)
                with dve.Fori(0, (KF - 6) // 2) as i:
                    tile(4, i, 0)
                    tile(5, i, 2)
                for t in (KF - 2, KF - 1):
                    for j in range(2):
                        c = 2 * (t - KF + 2) + j
                        split_lo(base + GATE_UP_UNITS + c, 0, DOWN_PARTS[c] * P)
                    evacuate(t, 0, 2 * (t % 2))

                def add_tile(d0, i):
                    dve.wait_ge(npost["sq"], i + (d0 + 1))
                    dve.wait_ge(npost["acc"], i + (d0 + 1))
                    nc.vector.tensor_tensor(acc_post[:, :], acc_post[:, :], sq[:, d0 % 2, :],
                                            ALU.add).then_inc(npost["acc"], 1)

                def down(d0, i, sizes, u0):
                    for c in range(3):
                        split_lo(u0 + c, i, sizes[c] * P)
                    add_tile(d0, i)
                    split_lo(u0 + 3, i, sizes[3] * P)

                u0 = base + GATE_UP_UNITS + 4
                with dve.Fori(0, (KD - 2) // 2) as i:
                    down(0, 2 * i, DOWN_PARTS, u0)
                    down(1, 2 * i, DOWN_PARTS, u0 + 4)
                down(KD - 2, 0, DOWN_PARTS, u0 + 4 * (KD - 2))
                if nnext is not None:
                    down(KD - 1, 0, (8,) * 4, next_base)
                else:
                    add_tile(KD - 1, 0)
                factor(npost, 2, 0.5)
                residual(npost, nnext, gnext)

            def scaled_tile(n, bank, scale, u):
                dve.wait_ge(w_used, MIX + u + 1)
                nc.vector.scalar_tensor_tensor(tmp[:, 2 + n % 2, :], ps[:, bank, :], scale, rsb[:, :], ALU.mult,
                                               ALU.mult).then_inc(proj_evac, 1)

            def low_part(n, dst_hi, dst_lo):
                dve.wait_ge(proj_hi, n + 1)
                nc.vector.tensor_tensor(dst_lo, tmp[:, 2 + n % 2, :], dst_hi.bitcast(F32), ALU.subtract).then_inc(proj_lo, 1)

            def roped_tile(n, bank, scale, u):
                dve.wait_ge(w_used, MIX + u + 1)
                nc.vector.scalar_tensor_tensor(tmp[:, 0, :], ps[:, bank, :], scale, cos, ALU.mult, ALU.mult)
                for a in range(4):
                    r, o = 32 * a, 32 * (a ^ 1)
                    last = nc.vector.scalar_tensor_tensor(tmp[o:o + 32, 1, :], ps[r:r + 32, bank, :], scale,
                                                          sin[r:r + 32, :], ALU.mult, ALU.mult)
                last.then_inc(proj_evac, 1)
                dve.wait_ge(proj_evac, 14 + n - 8)
                nc.vector.tensor_tensor(tmp[:, 2 + n % 2, :], tmp[:, 0, :], tmp[:, 1, :], ALU.add).then_inc(proj_val, 1)

            def fox_softmax(h):
                for b in range(TB):
                    dve.wait_ge(fox["score"], 4 * h + b + 1)
                    nc.vector.tensor_reduce(negmax[:, 0, b:b + 1], ps[:, b, 0:(b + 1) * P], AX.X, ALU.max,
                                            negate=True).then_inc(fox["max"], 1)
                for b in range(TB):
                    dve.wait_ge(fox["exp"], 4 * h + b + 1)
                    nc.vector.reciprocal(recip[:, 0, b:b + 1], rowsum[:, 0, b:b + 1]).then_inc(fox["rec"], 1)

            def swa_softmax(h):
                p = h % 2
                dve.wait_ge(swa["score"], h + 1)
                nc.vector.tensor_reduce(negmax[:, p, :],
                                        ps[:, 2 * p:2 * p + 2, :].rearrange("p a (b c) -> p (a b) c", b=2),
                                        AX.X, ALU.max, negate=True).then_inc(swa["rawmax"], 1)
                dve.wait_ge(swa["rawmax"], h + 1)
                nc.vector.tensor_scalar(negmax[:, p, :], negmax[:, p, :], nsink[:, h:h + 1], None,
                                        ALU.min).then_inc(swa["max"], 1)
                dve.wait_ge(swa["exp"], h + 1)
                nc.vector.tensor_tensor(rowsum[:, p, :], rowsum[:, p, :], sinkexp[:, p, :], ALU.add).then_inc(swa["sum"], 1)
                dve.wait_ge(swa["sum"], h + 1)
                nc.vector.reciprocal(recip[:, p, :], rowsum[:, p, :]).then_inc(swa["rec"], 1)

            def run_mixer():
                npre = pre[1]
                nc.vector.memset(acc_post[:, :], 0.0).then_inc(post[1]["acc"], 1)
                for j in range(4):
                    split_lo(MIX + 4 + j)
                factor(npre, 6, 1.0)
                dve.wait_ge(npre["rsb"], 1)
                for n in range(4):
                    scaled_tile(n, n, SCALE, Q_A + n)
                    low_part(n, h_hi[:, T_QA + n, :], h_lo[:, T_QA + n, :])
                nc.vector.tensor_tensor(cos, cos, rsb[:, :], ALU.mult)
                nc.vector.tensor_tensor(sin, sin, rsb[:, :], ALU.mult).then_inc(rope_scaled, 1)
                for t in range(4):
                    n = 4 + t
                    split_lo(MIX + K_A + t + 4)
                    scaled_tile(n, (4, 5, 0, 1)[t], 1.0, K_A + t)
                    low_part(n, h_hi[:, T_KA + t, :], h_lo[:, T_KA + t, :])
                split_lo(MIX + FG + 4)
                dve.wait_ge(w_used, MIX + FG + 1)
                z, a, zero = tmp[0:HEADS, 0, :], tmp[0:HEADS, 1, :], tmp[0:HEADS, 2, :]
                nc.vector.memset(zero, 0.0)
                nc.vector.tensor_tensor(z, ps[0:HEADS, 6, :], rsb[0:HEADS, :], ALU.mult).then_inc(proj_evac, 1)
                dve.wait_ge(proj_evac, 9)
                nc.vector.tensor_scalar(z, z, fbias[:, 0:1], None, ALU.add).then_inc(fgate, 2)
                dve.wait_ge(fgate, 2)
                nc.vector.scalar_tensor_tensor(a, z, -1.0, z, ALU.mult, ALU.min).then_inc(fgate, 1)
                dve.wait_ge(fgate_act, 2)
                nc.vector.scalar_tensor_tensor(a, z, 0.0, a, ALU.min, ALU.subtract).then_inc(rope_parts, 1)
                dve.wait_ge(rope_parts, 1)
                nc.vector.tensor_tensor_scan(z, a, zero, 0.0, ALU.add, ALU.add).then_inc(fgate, 1)
                dve.wait_ge(fgate_act, 4)
                for r in (0, DH):
                    last = nc.vector.scalar_tensor_tensor(cum_r[r + 32:r + 32 + HEADS, :], z, -1.0,
                                                          cum_r[0:HEADS, :].bitcast(F32), ALU.mult, ALU.subtract)
                last.then_inc(fgate, 1)
                for u in range(4):
                    split_lo(MIX + V_A + u + 4)
                for t in range(TB):
                    dve.wait_ge(v_hi_made, t + 1)
                    nc.vector.scalar_tensor_tensor(v_lo[:, t, 0:S], ps[:, 2 + t, :], rs[:, t:t + 1],
                                                   v_hi[:, t, 0:S].bitcast(F32), ALU.mult,
                                                   ALU.subtract).then_inc(proj_evac, 1)
                dve.wait_ge(rope_scaled, 1)
                for t in range(4):
                    split_lo(MIX + Q_B + t + 4)
                    roped_tile(8 + t, (0, 1, 6, 7)[t], SCALE, Q_B + t)
                    low_part(8 + t, h_hi[:, T_QB + t, :], h_lo[:, T_QB + t, :])
                split_lo(MIX + K_B + 4)
                roped_tile(12, 2, 1.0, K_B)
                low_part(12, h_hi[:, T_KB, :], h_lo[:, T_KB, :])
                split_lo(MIX + V_B + 4)
                dve.wait_ge(v_hi_made, 2 * TB)
                for t in range(TB):
                    last = nc.vector.scalar_tensor_tensor(v_lo[:, t, S:S + P], ps[:, 3, t * P:(t + 1) * P],
                                                          rs[:, t:t + 1], v_hi[:, t, S:S + P].bitcast(F32),
                                                          ALU.mult, ALU.subtract)
                last.then_inc(proj_evac, 1)

                fox_softmax(0)
                for h in range(HEADS):
                    for b in range(TB):
                        dve.wait_ge(fox["pth"], 4 * h + b + 1)
                        nc.vector.tensor_tensor(pt_lo[:, 0:b + 1, b * P:(b + 1) * P],
                                                ps[:, 4 + b % 2, 0:(b + 1) * P].rearrange("p (j q) -> p j q", q=P),
                                                pt_hi[:, 0:b + 1, b * P:(b + 1) * P].bitcast(F32),
                                                ALU.subtract).then_inc(fox["ptl"], 1)
                    if h + 1 < HEADS:
                        fox_softmax(h + 1)
                    else:
                        swa_softmax(0)
                    dve.wait_ge(fox["oh"], h + 1)
                    r = DH * (h % 2)
                    nc.vector.tensor_tensor(h_lo[r:r + DH, T_QA + h // 2, :], ps[r:r + DH, 6 + h % 2, :],
                                            h_hi[r:r + DH, T_QA + h // 2, :].bitcast(F32),
                                            ALU.subtract).then_inc(fox["ol"], 1)
                for h in range(HEADS):
                    for g, n in ((0, 512), (1, 384)):
                        dve.wait_ge(swa["pth"], 2 * h + g + 1)
                        nc.vector.tensor_tensor(ptb_lo[:, h % 2, 512 * g:512 * g + n], ps[:, 4 + g, 0:n],
                                                ptb_hi[:, h % 2, 512 * g:512 * g + n].bitcast(F32),
                                                ALU.subtract).then_inc(swa["ptl"], 1)
                    if h + 1 < HEADS:
                        swa_softmax(h + 1)
                    dve.wait_ge(swa["oh"], h + 1)
                    r = DH * (h % 2)
                    nc.vector.tensor_tensor(h_lo[r:r + DH, T_QB + h // 2, :], ps[r:r + DH, 6 + h % 2, :],
                                            h_hi[r:r + DH, T_QB + h // 2, :].bitcast(F32),
                                            ALU.subtract).then_inc(mix_evac, 1)

                with dve.Fori(0, KD // 4) as i:
                    for j in range(4):
                        u0 = MIX + GATES + 3 * j
                        b = 4 * (j % 2)
                        for g in range(2):
                            split_lo(u0 + 4 + g, 3 * i)
                            dve.wait_ge(w_used, 12 * i + (u0 + g + 1))
                            nc.vector.tensor_tensor(tmp[:, g, :], ps[:, b + g, :], rsb[:, :],
                                                    ALU.mult).then_inc(gate_scaled, 1)
                        split_lo(u0 + 6, 3 * i)
                        dve.wait_ge(w_used, 12 * i + (u0 + 3))
                        dve.wait_ge(gate_sig, 8 * i + (2 * j + 2))
                        nc.vector.tensor_tensor(tmp[:, 0, :], ps[:, b + 2, :], tmp[:, 0, :],
                                                ALU.mult).then_inc(branch_parts, 1)
                        nc.vector.tensor_tensor(tmp[:, 1, :], ps[:, b + 3, :], tmp[:, 1, :],
                                                ALU.mult).then_inc(mix_evac, 1)
                        dve.wait_ge(mix_evac, 4 * i + (HEADS + j + 1))
                        nc.vector.tensor_tensor(tmp[:, 2, :], tmp[:, 0, :], tmp[:, 1, :], ALU.add).then_inc(merged_val, 1)
                        dve.wait_ge(merged_hi, 4 * i + (j + 1))
                        at = bass.ds(4 * i + (T_MERGED + j), 1)
                        nc.vector.tensor_tensor(h_lo[:, at, :].rearrange("p a b -> p (a b)"), tmp[:, 2, :],
                                                h_hi[:, at, :].rearrange("p a b -> p (a b)").bitcast(F32),
                                                ALU.subtract).then_inc(merged_lo, 1)
                with dve.Fori(0, KD // 4) as i:
                    for j in range(4):
                        dve.wait_ge(post[1]["sq"], 4 * i + (j + 1))
                        dve.wait_ge(post[1]["acc"], 4 * i + (j + 1))
                        nc.vector.tensor_tensor(acc_post[:, :], acc_post[:, :], sq[:, j % 2, :],
                                                ALU.add).then_inc(post[1]["acc"], 1)
                        split_lo(MIX + OUT + j + 4, i)
                factor(post[1], 2, 1.0)
                residual(post[1], pre[2], 4)

            nc.vector.memset(ones[:, :], 1.0).then_inc(fills_made, 1)
            nc.vector.memset(half[:, :], -0.5).then_inc(fills_made, 1)
            nc.vector.memset(cum_r[:, :].bitcast(F32), 0.0).then_inc(fills_made, 1)
            for j in range(KD // 2):
                low_input(2 * j, pre[0], 0)
                low_input(2 * j + 1, pre[0], 0)
                split_lo(FFN1 + j)
            dve.wait_ge(small_loaded, 64)
            nc.vector.tensor_scalar(nsink[:, :], sink[:, :], -1.0, None, ALU.mult)
            run_ffn(FFN1, ffn[0], pre[0], post[0], pre[1], 2, MIX)
            run_mixer()
            run_ffn(FFN2, ffn[1], pre[2], post[2], None, None, None)

        @block.gpsimd
        def _(pool):
            def pre_squares(n):
                nc.gpsimd.memset(acc_pre[:, :], 0.0).then_inc(n["acc"], 1)
                for k in range(KD):
                    pool.wait_ge(n["sq"], k + 1)
                    pool.wait_ge(n["acc"], k + 1)
                    nc.gpsimd.tensor_tensor(acc_pre[:, :], acc_pre[:, :], sq[:, k % 2, :], ALU.add).then_inc(n["acc"], 1)

            def power(n):
                pool.wait_ge(n["ms"], 1)
                nc.gpsimd.tensor_tensor(rs[:, :], ms[:, :], half[:, :], ALU.pow).then_inc(n["rs"], 1)

            pool.wait_ge(fills_made, 3)
            pre_squares(pre[0])
            power(pre[0])
            power(post[0])
            pre_squares(pre[1])
            power(pre[1])
            for h in range(HEADS):
                for b in range(TB):
                    pool.wait_ge(fox["rec"], 4 * h + b + 1)
                    n = (b + 1) * P
                    nc.gpsimd.tensor_scalar(tmp[:, b, 0:n], tmp[:, b, 0:n], recip[:, 0, b:b + 1], None,
                                            ALU.mult).then_inc(fox["norm"], 1)
            for h in range(HEADS):
                pool.wait_ge(swa["rec"], h + 1)
                nc.gpsimd.tensor_tensor(pb[:, h % 2], pb[:, h % 2],
                                        recip[:, h % 2, :].unsqueeze(2).to_broadcast([P, TB, 2 * P]),
                                        ALU.mult).then_inc(swa["norm"], 1)
            power(post[1])
            pre_squares(pre[2])
            power(pre[2])
            power(post[2])


def tiles(w, rows):
    return w.reshape(rows, P, -1, P).transpose(2, 1, 0, 3).reshape(-1, P, rows * P)


def kernel(**inputs):
    import concourse.bacc as _bacc
    from concourse.bass_utils import run_bass_kernel_spmd as _run

    a = {k: np.asarray(v) for k, v in inputs.items()}

    def gate_up(n):
        g, u = tiles(a[f"ffn{n}_w_gate"][0], KD), tiles(a[f"ffn{n}_w_up"][0], KD)
        return np.ascontiguousarray(np.stack([g, u], axis=1).reshape(-1, P, UNIT))

    w_in = a["w_in"][0]
    fox = HEADS * DH
    cuts = np.cumsum([0, fox, fox, fox, HEADS, fox, P, P, D, D])
    q_a, k_a, v_a, f_a, q_b, k_b, v_b, gate_a, gate_b = (w_in[:, s:e] for s, e in zip(cuts[:-1], cuts[1:]))
    order = np.arange(HEADS).reshape(2, HEADS // 2).T.reshape(-1)
    q_b = q_b.reshape(D, HEADS, DH)[:, order].reshape(D, fox)
    w_swa = a["w_branch_swa"][0].reshape(HEADS, DH, D)[order].reshape(fox, D)
    f_wide = w_in[:, cuts[3]:cuts[3] + P]
    v_units = v_a.reshape(4, 2, P, fox).transpose(0, 2, 1, 3).reshape(4, P, UNIT)
    branch = np.concatenate([tiles(a["w_branch_fox"][0], 4), tiles(w_swa, 4)], axis=2)
    gates = np.stack([tiles(gate_a, KD), tiles(gate_b, KD), branch], axis=1).reshape(-1, P, UNIT)
    mixw = np.concatenate([tiles(q_a, KD), tiles(k_a, KD), tiles(f_wide, KD), v_units, tiles(q_b, KD),
                           tiles(k_b, KD), tiles(v_b, KD), gates, tiles(a["w_out"][0], KD)], axis=0)

    gains = np.stack([a[n][0].reshape(KD, P).T for n in ("ffn1_pre_g", "ffn1_post_g", "mix_pre_g", "mix_post_g",
                                                         "ffn2_pre_g", "ffn2_post_g")], axis=1)
    sinks = np.broadcast_to(a["swa_sinks"][0][order], (P, HEADS))

    i = np.arange(P)
    before = np.where(i[None, :] > i[:, None], 0.0, MASKED)
    same = np.where(i[None, :] <= i[:, None], 0.0, MASKED)
    pick = ((i[:, None] % 32 == np.arange(HEADS)[None, :]) & (i[:, None] % DH < 40)).astype(np.float32)
    consts = np.concatenate([np.eye(P), before, same, np.full((P, P), MASKED), pick], axis=1).astype(np.float32)
    inv = (np.float32(1.0) / np.float32(10000.0) ** (np.arange(0, DH, 2, dtype=np.float32) / np.float32(DH)))
    ang = (np.arange(S, dtype=np.float32)[:, None] * inv.astype(np.float32)[None, :]).T
    cos, sin = np.cos(ang), np.sin(ang)
    rope = np.stack([np.tile(cos, (4, 1)), np.tile(np.concatenate([sin, -sin]), (2, 1))], axis=1).astype(np.float32)

    arrays = {
        "x_in": a["x"][0].T.reshape(KD, P, S).transpose(1, 0, 2),
        "gu1": gate_up(1), "dn1": tiles(a["ffn1_w_down"][0], KF), "mixw": mixw,
        "gu2": gate_up(2), "dn2": tiles(a["ffn2_w_down"][0], KF), "gains": gains, "sinks": sinks,
        "forget_bias": a["fox_forget_bias"][0].reshape(HEADS, 1), "consts": consts, "rope": rope,
    }
    arrays = {k: np.ascontiguousarray(v) for k, v in arrays.items()}

    nc = _bacc.Bacc("TRN2", target_bir_lowering=False, num_devices=1, dynamic_dma_scratch_size=1024)
    args = [nc.dram_tensor(k, v.shape, F32, kind="ExternalInput").ap() for k, v in arrays.items()]
    out = nc.dram_tensor("out", (P, KD, S), F32, kind="ExternalOutput").ap()
    build(nc, *args, out)
    r = _run(nc, [arrays], core_ids=[0])
    got = np.asarray(r.results[0]["out"])
    return np.ascontiguousarray(got.transpose(1, 0, 2).reshape(D, S).T)[None]
```

```python
from contextlib import ExitStack

import numpy as np
import concourse.bass as bass
from concourse import mybir

F32 = mybir.dt.float32
F32R = mybir.dt.float32r
ACT = mybir.ActivationFunctionType
ALU = mybir.AluOpType
AX = mybir.AxisListType

P = 128
D = 1024
S = 512
F = 2816
DH = 64
HEADS = 8
KD = D // P
KF = F // P
TB = S // P
EPS = 1e-6
SCALE = DH ** -0.5
MASKED = -(2.0 ** 126)

DVE_TILES = 6

RING = 4
UNIT = 8 * P
DOWN_PARTS = (6, 5, 6, 5)
DOWN_FROM = (0, 6, 11, 17)

X_PARTS = ((0,), (1,), (2, 3), (4, 5), (6, 7))

GATE_UP_UNITS = 2 * KF
DOWN_UNITS = 4 * KD
FFN_UNITS = GATE_UP_UNITS + DOWN_UNITS
Q_A, K_A, FG, Q_B, K_B, V_A, V_B = 0, 4, 8, 9, 13, 14, 18
GATES = 19
BRANCH = GATES + 2 * KD
OUT = BRANCH + KD
MIX_UNITS = OUT + KD
FFN1, MIX, FFN2 = 0, FFN_UNITS, FFN_UNITS + MIX_UNITS

T_QA, T_QB, T_KA, T_KB, T_V, T_PT = 0, 4, 8, 12, 13, 18
T_MERGED = 8
V_BANKS = (4, 5, 6, 2)


def build(nc, x_in, gu1, dn1, mixw, gu2, dn2, gains, sinks, forget_bias, consts, rope, x_kept, out):
    with ExitStack() as ctx:
        def sb(name, shape, dt=F32):
            return ctx.enter_context(nc.sbuf_tensor(name, shape, dt))

        def sem(name):
            return ctx.enter_context(nc.semaphore(name))

        xs_hi = sb("xs_hi", [P, KD, S], F32R)
        xs_lo_at = -(-nc.sbuf_base // 32) * 32
        xs_lo = sb("xs_lo", [P, KD, S], F32R)
        h_hi = sb("h_hi", [P, KF, S], F32R)
        h_lo = sb("h_lo", [P, KF, S], F32R)
        w_hi = sb("w_hi", [P, RING, UNIT], F32R)
        w_lo = sb("w_lo", [P, RING, UNIT], F32R)
        ident_r = sb("ident_r", [P, P], F32R)
        mask_r = sb("mask_r", [P, 3, P], F32R)
        pick_r = sb("pick_r", [P, HEADS], F32R)
        cum_r = sb("cum_r", [P, S], F32R)
        x = sb("x", [P, KD, S])
        raw = sb("raw", [P, RING, UNIT])
        tmp = sb("tmp", [P, 4, S])
        gate_b = sb("gate_b", [P, KD, S])
        rsb = sb("rsb", [P, S])
        cst = sb("cst", [P, 4 * P + HEADS])
        ones = sb("ones", [P, P])
        gain = sb("gain", [P, 6, KD])
        sink = sb("sink", [P, HEADS])
        nsink = sb("nsink", [P, HEADS])
        fbias = sb("fbias", [HEADS, 1])
        ms = sb("ms", [P, TB])
        rs = sb("rs", [P, TB])
        half = sb("half", [P, TB])
        negmax = sb("negmax", [P, 2, TB])
        rowsum = sb("rowsum", [P, 2, TB])
        sinkexp = sb("sinkexp", [P, 2, TB])
        recip = sb("recip", [P, 2, TB])
        y = nc.alloc_sbuf_tensor_at("y", [P, KD, S], F32, offset=xs_lo_at)
        ps = ctx.enter_context(nc.psum_tensor("ps", [P, 8, S], F32))

        ident = cst[:, 0:P]
        ropes = gate_b[:, 0:2, :]
        cos, sin = gate_b[:, 0, :], gate_b[:, 1, :]
        sq, acc_pre, acc_post = gate_b[:, 4:6, :], gate_b[:, 6, :], gate_b[:, 7, :]
        v_hi = h_hi[:, T_V:T_V + 5, :].rearrange("p a b -> p (a b)").rearrange("p (t c) -> p t c", t=TB)
        v_lo = h_lo[:, T_V:T_V + 5, :].rearrange("p a b -> p (a b)").rearrange("p (t c) -> p t c", t=TB)
        pt_hi, pt_lo = h_hi[:, T_PT:T_PT + 4, :], h_lo[:, T_PT:T_PT + 4, :]
        ptb_hi = pt_hi.rearrange("p a b -> p (a b)").rearrange("p (u c) -> p u c", u=2)
        ptb_lo = pt_lo.rearrange("p a b -> p (a b)").rearrange("p (u c) -> p u c", u=2)
        pb = tmp[:, :, :].rearrange("p a b -> p (a b)").rearrange("p (u b c) -> p u b c", u=2, b=TB)

        w_loaded = [sem(f"w_loaded{i}") for i in range(RING)]
        w_hi_made = sem("w_hi_made")
        w_lo_made = sem("w_lo_made")
        w_used = sem("w_used")
        small_loaded = sem("small_loaded")
        gain_loaded = sem("gain_loaded")
        x_loaded = [sem(f"x_loaded{i}") for i in range(len(X_PARTS))]
        fills_made = sem("fills_made")
        half_made = sem("half_made")
        consts_split = sem("consts_split")
        pre = [{n: sem(f"pre{i}_{n}") for n in ("hi", "lo", "sq", "acc", "ss", "ms", "rs", "diag", "bc", "rsb")}
               for i in range(3)]
        post = [{n: sem(f"post{i}_{n}") for n in ("sq", "acc", "ss", "ms", "rs", "diag", "bc", "t", "x")}
                for i in range(3)]
        ffn = [{n: sem(f"ffn{i}_{n}") for n in ("scaled", "silu", "prod", "hi", "lo", "evac")} for i in range(2)]
        proj_evac = sem("proj_evac")
        proj_val = sem("proj_val")
        proj_hi = sem("proj_hi")
        proj_lo = sem("proj_lo")
        v_hi_made = sem("v_hi_made")
        rope_scaled = sem("rope_scaled")
        rope_parts = sem("rope_parts")
        fgate = sem("fgate")
        fgate_act = sem("fgate_act")
        fox = {n: sem(f"fox_{n}") for n in ("score", "max", "exp", "rec", "norm", "tr", "pth", "ptl", "pv", "oh", "ol")}
        swa = {n: sem(f"swa_{n}") for n in ("score", "rawmax", "max", "exp", "sum", "rec", "norm", "tr", "pth", "ptl",
                                            "pv", "oh")}
        mix_evac = sem("mix_evac")
        x_saved = sem("x_saved")
        x_back = sem("x_back")
        gate_evac = sem("gate_evac")
        gate_sig = sem("gate_sig")
        branch_parts = sem("branch_parts")
        merged_val = sem("merged_val")
        merged_hi = sem("merged_hi")
        merged_lo = sem("merged_lo")
        last_factor = sem("last_factor")
        pool_scaled = sem("pool_scaled")
        pool_summed = sem("pool_summed")
        stored = sem("stored")

        block = ctx.enter_context(nc.Block())

        def loads_of(u0):
            return u0 % RING, 16 * (u0 // RING + 1)

        @block.sync
        def _(sp):
            def load(u0, i, src, elems):
                if not (isinstance(i, int) and u0 + RING * i < RING):
                    sp.wait_ge(w_lo_made, RING * i + (u0 - RING + 1))
                sp.dma_start(raw[:, u0 % RING, 0:elems], src).then_inc(w_loaded[u0 % RING], 16)

            def ffn_loads(base, gu, dn, first):
                def x_load(j):
                    a, b = X_PARTS[j][0], X_PARTS[j][-1] + 1
                    sp.dma_start(x[:, a:b, :], x_in[:, a:b, :]).then_inc(x_loaded[j], 16)

                if first:
                    x_load(0)
                load(base, 0, gu[0], UNIT)
                load(base + 1, 0, gu[1], UNIT)
                if first:
                    for j in range(1, len(X_PARTS)):
                        x_load(j)
                load(base + 2, 0, gu[2], UNIT)
                load(base + 3, 0, gu[3], UNIT)
                if first:
                    sp.dma_start(cst[:, :], consts).then_inc(small_loaded, 16)
                    sp.dma_start(ropes, rope).then_inc(small_loaded, 16)
                    sp.dma_start(sink[:, :], sinks).then_inc(small_loaded, 16)
                    sp.dma_start(fbias[:, :], forget_bias).then_inc(small_loaded, 16)
                with sp.Fori(1, GATE_UP_UNITS // RING) as i:
                    for j in range(RING):
                        load(base + j, i, gu[bass.ds(RING * i + j, 1)].rearrange("a p n -> (a p) n"), UNIT)
                with sp.Fori(0, KD) as d:
                    for c in range(4):
                        n, at = DOWN_PARTS[c] * P, DOWN_FROM[c] * P
                        load(base + GATE_UP_UNITS + c, d,
                             dn[bass.ds(d, 1), :, at:at + n].rearrange("a p n -> (a p) n"), n)

            sp.dma_start(gain[:, :, :], gains).then_inc(gain_loaded, 16)
            ffn_loads(FFN1, gu1, dn1, True)
            for u in range(2 * RING):
                load(MIX + u, 0, mixw[u], UNIT)
            sp.wait_ge(post[0]["x"], KD)
            sp.dma_start(x_kept, x[:, :, :]).then_inc(x_saved, 16)
            with sp.Fori(0, (OUT - 2 * RING) // RING) as i:
                for j in range(RING):
                    u = 2 * RING + j
                    load(MIX + u, i, mixw[bass.ds(RING * i + u, 1)].rearrange("a p n -> (a p) n"), UNIT)
            for u in range(OUT // RING * RING, OUT):
                load(MIX + u, 0, mixw[u], UNIT)
            sp.wait_ge(x_saved, 16)
            for k in range(KD):
                load(MIX + OUT + k, 0, mixw[OUT + k], UNIT)
                sp.wait_ge(merged_val, k + 1)
                sp.dma_start(x[:, k, :], x_kept[:, k, :]).then_inc(x_back, 16)
            ffn_loads(FFN2, gu2, dn2, False)
            for k in (0, 1, 2, 6, 3, 4, 7, 5):
                if k < DVE_TILES:
                    sp.wait_ge(post[2]["x"], k + 1)
                else:
                    sp.wait_ge(pool_summed, k - DVE_TILES + 1)
                sp.dma_start(out[:, k, :], x[:, k, :]).then_inc(stored, 16)
            sp.wait_ge(stored, 16 * KD)

        @block.tensor
        def _(pe):
            def product(o, st, mv, first=False, last=False):
                nc.tensor.matmul(o, st[0], mv[0], start=first, stop=False, skip_group_check=True)
                nc.tensor.matmul(o, st[0], mv[1], start=False, stop=False, skip_group_check=True)
                return nc.tensor.matmul(o, st[1], mv[0], start=False, stop=last, skip_group_check=True)

            def wblock(u0, k, width=P):
                s = u0 % RING
                return w_hi[:, s, k * width:(k + 1) * width], w_lo[:, s, k * width:(k + 1) * width]

            def xtile(k, a=0, b=S):
                return xs_hi[:, k, a:b], xs_lo[:, k, a:b]

            def htile(k, a=0, b=S):
                return h_hi[:, k, a:b], h_lo[:, k, a:b]

            def sum_squares(n):
                pe.wait_ge(n["acc"], KD + 1)
                for t in range(TB):
                    last = nc.tensor.matmul(ps[:, 6, t:t + 1], acc_pre[:, t * P:(t + 1) * P], ones[:, 0:1],
                                            start=True, stop=True)
                last.then_inc(n["ss"], 1)

            def sum_result_squares(n):
                pe.wait_ge(n["acc"], KD)
                for t in range(TB):
                    nc.tensor.matmul(ps[:, 2, t:t + 1], acc_post[:, t * P:(t + 1) * P], ones[:, 0:1],
                                     start=(t == 0), stop=False, skip_group_check=True)
                pe.wait_ge(n["sq"], KD)
                for t in range(TB):
                    last = nc.tensor.matmul(ps[:, 2, t:t + 1], sq[:, 1, t * P:(t + 1) * P], ones[:, 0:1],
                                            start=False, stop=True, skip_group_check=True)
                last.then_inc(n["ss"], 1)

            def broadcast_factor(n, bank):
                pe.wait_ge(n["diag"], 1)
                nc.tensor.matmul(ps[:, bank, :], ones[:, :], tmp[:, 3, :], start=True, stop=True).then_inc(n["bc"], 1)

            def first_group(base, n, width):
                for k in range(KD // 2):
                    pe.wait_ge(n["lo"], k + 1)
                    for j in range(width):
                        if k == 0:
                            pe.wait_ge(w_lo_made, base + j + 1)
                        product(ps[:, j, :], wblock(base + j, k), xtile(k), first=(k == 0))
                for j in range(width):
                    for k in range(KD // 2, KD):
                        if j == 0:
                            pe.wait_ge(n["lo"], k + 1)
                        last = product(ps[:, j, :], wblock(base + j, k), xtile(k), last=(k == KD - 1))
                    last.then_inc(w_used, 1)

            def project(u0, i, bank):
                pe.wait_ge(w_lo_made, RING * i + (u0 + 1))
                for k in range(KD):
                    last = product(ps[:, bank, :], wblock(u0, k), xtile(k), first=(k == 0), last=(k == KD - 1))
                last.then_inc(w_used, 1)

            def post_norm(n):
                sum_result_squares(n)
                broadcast_factor(n, 5)
                if n is post[2]:
                    broadcast_factor(n, 7)

            def run_ffn(base, f, npre, npost):
                if base == FFN1:
                    first_group(base, npre, 2)
                    project(base + 2, 0, 2)
                    project(base + 3, 0, 3)
                else:
                    first_group(base, npre, 4)
                sum_squares(npre)
                project(base + 4, 0, 4)
                broadcast_factor(npre, 7)
                project(base + 5, 0, 5)

                def tile(t, i):
                    pe.wait_ge(f["evac"], 2 * i + (t - 1))
                    b = 2 * (t % 2)
                    project(base + 2 * t, i, b)
                    project(base + 2 * t + 1, i, b + 1)

                tile(3, 0)
                with pe.Fori(0, (KF - 4) // 2) as i:
                    tile(4, i)
                    tile(5, i)
                with pe.Fori(0, KD // 2) as i:
                    for j in range(2):
                        pe.wait_ge(f["evac"], 2 * i + (KF - 1 + j))
                        for c in range(4):
                            u0 = base + GATE_UP_UNITS + 4 * j + c
                            pe.wait_ge(w_lo_made, 8 * i + (u0 + 1))
                            pe.wait_ge(f["lo"], DOWN_FROM[c] + DOWN_PARTS[c])
                            for k in range(DOWN_PARTS[c]):
                                t = DOWN_FROM[c] + k
                                last = product(ps[:, j, :], wblock(u0, k), htile(t), first=(t == 0), last=(t == KF - 1))
                            last.then_inc(w_used, 1)
                post_norm(npost)

            def gate_half(v, half):
                u0 = MIX + GATES + v
                if half == 0:
                    pe.wait_ge(w_lo_made, u0 + 1)
                    if v:
                        pe.wait_ge(gate_evac, v)
                for k in range(4 * half, 4 * half + 4):
                    last = product(ps[:, 7, :], wblock(u0, k), xtile(k), first=(k == 0), last=(k == KD - 1))
                if half:
                    last.then_inc(w_used, 1)

            def fox_masks(h):
                for b in range(TB):
                    if h:
                        pe.wait_ge(fox["exp"], 4 * (h - 1) + b + 1)
                    nc.tensor.matmul(ps[:, b, b * P:(b + 1) * P], ident_r[:, :], mask_r[:, 1, :],
                                     start=True, stop=False, skip_group_check=True)

            def fox_scores(h, blocks):
                r = DH * (h % 2)
                q, k = T_QA + h // 2, T_KA + h // 2
                for b in blocks:
                    n = (b + 1) * P
                    o = ps[:, b, 0:n]
                    nc.tensor.matmul(o, pick_r[r:r + 40, h:h + 1].to_broadcast([40, P]), cum_r[r:r + 40, 0:n],
                                     start=False, stop=False, skip_group_check=True)
                    product(o, (h_hi[r:r + DH, q, b * P:n], h_lo[r:r + DH, q, b * P:n]),
                            (h_hi[r:r + DH, k, 0:n], h_lo[r:r + DH, k, 0:n]), last=True).then_inc(fox["score"], 1)

            def fox_transpose(h, blocks):
                for b in blocks:
                    pe.wait_ge(fox["norm"], 4 * h + b + 1)
                    if 4 * h + b >= 2:
                        pe.wait_ge(fox["ptl"], 4 * h + b - 1)
                    for j in range(b + 1):
                        last = nc.tensor.transpose(ps[:, 4 + b % 2, j * P:(j + 1) * P], tmp[:, b, j * P:(j + 1) * P],
                                                   ident)
                    last.then_inc(fox["tr"], 1)

            def fox_values(h):
                pe.wait_ge(fox["ptl"], 4 * (h + 1))
                if h:
                    pe.wait_ge(fox["ol"], h)
                c = P * (h // 2)
                for j in range(TB):
                    last = product(ps[:, 6, j * P:S], (v_hi[:, j, c:c + P], v_lo[:, j, c:c + P]),
                                   (pt_hi[:, j, j * P:S], pt_lo[:, j, j * P:S]), first=(j == 0), last=(j == TB - 1))
                last.then_inc(fox["pv"], 1)

            def swa_scores(h):
                r = DH * (h % 2)
                q = T_QB + h // 2
                if h == 0:
                    pe.wait_ge(fox["exp"], 4 * HEADS)
                elif h >= 2:
                    pe.wait_ge(swa["exp"], h - 1)
                def place(b):
                    return ps[:, 2 * (h % 2) + b // 2, 256 * (b % 2):256 * (b % 2) + 256]

                for b in range(TB):
                    if b == 0:
                        nc.tensor.matmul(place(b)[:, 0:P], ident_r[:, :], mask_r[:, 2, :],
                                         start=True, stop=False, skip_group_check=True)
                        nc.tensor.matmul(place(b)[:, P:2 * P], ident_r[:, :], mask_r[:, 1, :],
                                         start=False, stop=False, skip_group_check=True)
                    else:
                        nc.tensor.matmul(place(b), ident_r[:, :], mask_r[:, 0:2, :].rearrange("p a b -> p (a b)"),
                                         start=(b % 2 == 0), stop=False, skip_group_check=True)
                for b in range(TB):
                    k0, k1 = max(0, b - 1) * P, (b + 1) * P
                    last = product(place(b)[:, 2 * P - (k1 - k0):2 * P],
                                   (h_hi[r:r + DH, q, b * P:k1], h_lo[r:r + DH, q, b * P:k1]),
                                   (h_hi[r:r + DH, T_KB, k0:k1], h_lo[r:r + DH, T_KB, k0:k1]), last=True)
                last.then_inc(swa["score"], 1)

            def swa_transpose(h):
                pe.wait_ge(swa["norm"], h + 1)
                if h == 0:
                    pe.wait_ge(fox["ptl"], 4 * HEADS)
                else:
                    pe.wait_ge(swa["ptl"], 2 * h)
                for j in range(TB):
                    o = ps[:, 4 + j // 2, 256 * (j % 2):256 * (j % 2) + 256]
                    last = nc.tensor.transpose(o[:, 0:P], pb[:, h % 2, j, P:2 * P], ident)
                    if j < TB - 1:
                        last = nc.tensor.transpose(o[:, P:2 * P], pb[:, h % 2, j + 1, 0:P], ident)
                    if j % 2:
                        last.then_inc(swa["tr"], 1)

            def swa_values(h):
                pe.wait_ge(swa["ptl"], 2 * (h + 1))
                if h == 0:
                    pe.wait_ge(fox["ol"], HEADS)
                else:
                    pe.wait_ge(mix_evac, h)
                c = P * (HEADS // 2)
                for j in range(TB):
                    n = min(2 * P, S - j * P)
                    last = product(ps[:, 6, j * P:j * P + n], (v_hi[:, j, c:c + P], v_lo[:, j, c:c + P]),
                                   (ptb_hi[:, h % 2, 256 * j:256 * j + n], ptb_lo[:, h % 2, 256 * j:256 * j + n]),
                                   first=(j == 0), last=(j == TB - 1))
                last.then_inc(swa["pv"], 1)

            def branch_a(d):
                pe.wait_ge(w_lo_made, MIX + BRANCH + d + 1)
                if d == 0:
                    pe.wait_ge(fox["ol"], HEADS)
                for k in range(4):
                    product(ps[:, 2 * (d % 2), :], wblock(MIX + BRANCH + d, k), htile(T_QA + k),
                            first=(k == 0), last=(k == 3))

            def branch_b(d):
                for k in range(4):
                    if d == 0 and k == 3:
                        pe.wait_ge(mix_evac, HEADS)
                    last = product(ps[:, 2 * (d % 2) + 1, :], wblock(MIX + BRANCH + d, 4 + k), htile(T_QB + k),
                                   first=(k == 0), last=(k == 3))
                last.then_inc(w_used, 1)

            def run_mixer():
                npre = pre[1]
                first_group(MIX + Q_A, npre, 4)
                sum_squares(npre)
                project(MIX + K_A, 0, 4)
                broadcast_factor(npre, 7)
                project(MIX + K_A + 1, 0, 5)
                for t in (2, 3):
                    pe.wait_ge(proj_evac, t - 1)
                    project(MIX + K_A + t, 0, t - 2)
                project(MIX + FG, 0, 6)
                for t, (bank, n) in enumerate(((2, 3), (3, 4), (0, 7), (1, 8))):
                    pe.wait_ge(proj_evac, n)
                    project(MIX + Q_B + t, 0, bank)
                project(MIX + K_B, 0, 7)
                pe.wait_ge(proj_evac, 10)
                for u in range(4):
                    pe.wait_ge(w_lo_made, MIX + V_A + u + 1)
                    for kk in range(2):
                        k = 2 * u + kk
                        for t in range(TB):
                            last = product(ps[:, V_BANKS[t], :], xtile(k, t * P, (t + 1) * P),
                                           wblock(MIX + V_A + u, kk, S), first=(k == 0), last=(k == KD - 1))
                    last.then_inc(w_used, 1)
                pe.wait_ge(proj_evac, 11)
                pe.wait_ge(w_lo_made, MIX + V_B + 1)
                for t in range(TB):
                    for k in range(KD):
                        last = product(ps[:, 3, t * P:(t + 1) * P], xtile(k, t * P, (t + 1) * P),
                                       wblock(MIX + V_B, k), first=(k == 0), last=(k == KD - 1))
                last.then_inc(w_used, 1)

                pe.wait_ge(proj_evac, 14)
                gate_half(0, 0)
                gate_half(0, 1)
                pe.wait_ge(proj_evac, 19)
                pe.wait_ge(proj_lo, 13)
                pe.wait_ge(fgate, 5)
                pe.wait_ge(consts_split, 1)
                fox_masks(0)
                fox_scores(0, range(TB))
                gate_half(1, 0)
                gate_half(1, 1)
                for h in range(HEADS):
                    if h + 1 < HEADS:
                        fox_transpose(h, (0, 1))
                        fox_masks(h + 1)
                        fox_scores(h + 1, (0, 1))
                        fox_transpose(h, (2,))
                        fox_scores(h + 1, (2,))
                        fox_transpose(h, (3,))
                        fox_scores(h + 1, (3,))
                    else:
                        fox_transpose(h, range(TB))
                        swa_scores(0)
                    gate_half(h + 2, 0)
                    fox_values(h)
                    gate_half(h + 2, 1)
                for h in range(HEADS):
                    if h + 1 < HEADS:
                        swa_scores(h + 1)
                    else:
                        branch_a(0)
                    swa_transpose(h)
                    if h < HEADS - 3:
                        gate_half(HEADS + h + 2, 0)
                        swa_values(h)
                        gate_half(HEADS + h + 2, 1)
                    elif h < HEADS - 1:
                        gate_half(2 * HEADS - 1, h - (HEADS - 3))
                        swa_values(h)
                    else:
                        branch_a(1)
                        swa_values(h)

                for d in range(KD):
                    if d >= 2:
                        pe.wait_ge(mix_evac, HEADS + d - 1)
                        branch_a(d)
                    branch_b(d)
                with pe.Fori(0, KD // 4) as i:
                    for j in range(4):
                        pe.wait_ge(mix_evac, 4 * i + (HEADS + KD - 1 + j))
                        u0 = MIX + OUT + j
                        pe.wait_ge(w_lo_made, 4 * i + (u0 + 1))
                        pe.wait_ge(merged_lo, KD - 1)
                        for k in range(KD):
                            if k == KD - 1:
                                pe.wait_ge(merged_lo, KD)
                            last = product(ps[:, j % 2, :], wblock(u0, k), htile(T_MERGED + k),
                                           first=(k == 0), last=(k == KD - 1))
                        last.then_inc(w_used, 1)
                post_norm(post[1])

            pe.wait_ge(fills_made, 1)
            run_ffn(FFN1, ffn[0], pre[0], post[0])
            run_mixer()
            run_ffn(FFN2, ffn[1], pre[2], post[2])

        @block.scalar
        def _(act):
            def split_hi(u0, i=0, elems=UNIT):
                s, n = loads_of(u0)
                act.wait_ge(w_loaded[s], 16 * i + n)
                if not (isinstance(i, int) and u0 + RING * i < RING):
                    act.wait_ge(w_used, RING * i + (u0 - RING + 1))
                nc.scalar.activation(w_hi[:, s, 0:elems], raw[:, s, 0:elems], ACT.Copy).then_inc(w_hi_made, 1)

            def copy_factor(n):
                act.wait_ge(n["bc"], 1)
                nc.scalar.activation(rsb[:, :], ps[:, 7, :], ACT.Copy).then_inc(n["rsb"], 1)

            def high_input(k, n, g):
                nc.scalar.activation(xs_hi[:, k, :], x[:, k, :], ACT.Copy, scale=gain[:, g, k:k + 1]).then_inc(n["hi"], 1)

            def square_input(k, n):
                if k >= 2:
                    act.wait_ge(n["acc"], k)
                nc.scalar.activation(sq[:, k % 2, :], x[:, k, :], ACT.Square).then_inc(n["sq"], 1)

            def result_tile(d0, i, bank, n, g, used, evac, unit=None, at=0, elems=UNIT):
                d = i + d0
                act.wait_ge(w_used, used)
                act.wait_ge(n["acc"], d + 1)
                nc.scalar.activation(sq[:, d0 % 2, :], ps[:, bank, :], ACT.Square).then_inc(n["sq"], 1)
                if unit is not None:
                    split_hi(unit, at, elems)
                nc.scalar.activation(y[:, bass.ds(d, 1), :].rearrange("p a b -> p (a b)"), ps[:, bank, :], ACT.Copy,
                                     scale=gain[:, g, bass.ds(d, 1)]).then_inc(evac, 1)

            def next_input(npost, nnext, g):
                for k in range(KD):
                    act.wait_ge(npost["x"], k + 1)
                    high_input(k, nnext, g)
                    square_input(k, nnext)

            def run_ffn(base, f, npre, npost, gpost, nnext, gnext, next_base):
                for j in range(4):
                    split_hi(base + 4 + j)
                copy_factor(npre)

                def activate(t, i=0):
                    act.wait_ge(f["scaled"], i + (t + 1))
                    nc.scalar.activation(tmp[:, 0, :], tmp[:, 0, :], ACT.Silu).then_inc(f["silu"], 1)
                    act.wait_ge(f["prod"], i + (t + 1))
                    nc.scalar.activation(h_hi[:, bass.ds(i + t, 1), :].rearrange("p a b -> p (a b)"), tmp[:, 2, :],
                                         ACT.Copy).then_inc(f["hi"], 1)

                activate(0)
                activate(1)

                def tile(t, i):
                    for j in range(2):
                        split_hi(base + 2 * t + 4 + j, i)
                    activate(t, 2 * i)

                with act.Fori(0, (KF - 4) // 2) as i:
                    tile(2, i)
                    tile(3, i)
                for t in (KF - 2, KF - 1):
                    for j in range(2):
                        c = 2 * (t - KF + 2) + j
                        split_hi(base + GATE_UP_UNITS + c, 0, DOWN_PARTS[c] * P)
                    activate(t)

                def down(d0, i, sizes, u0):
                    used = 4 * i + (base + GATE_UP_UNITS + 4 * d0 + 4)
                    for c in range(3):
                        split_hi(u0 + c, i, sizes[c] * P)
                    result_tile(d0, i, d0 % 2, npost, gpost, used, f["evac"], u0 + 3, i, sizes[3] * P)

                u0 = base + GATE_UP_UNITS + 4
                with act.Fori(0, (KD - 2) // 2) as i:
                    down(0, 2 * i, DOWN_PARTS, u0)
                    down(1, 2 * i, DOWN_PARTS, u0 + 4)
                down(KD - 2, 0, DOWN_PARTS, u0 + 4 * (KD - 2))
                if nnext is not None:
                    down(KD - 1, 0, (8,) * 4, next_base)
                else:
                    result_tile(KD - 1, 0, (KD - 1) % 2, npost, gpost, base + FFN_UNITS, f["evac"])
                if nnext is not None:
                    next_input(npost, nnext, gnext)

            def high_part(n, dst):
                if n < 8:
                    act.wait_ge(proj_evac, n + 1)
                else:
                    act.wait_ge(proj_val, n - 7)
                nc.scalar.activation(dst, tmp[:, 2 + n % 2, :], ACT.Copy).then_inc(proj_hi, 1)

            def fox_exp(h, blocks):
                for b in blocks:
                    act.wait_ge(fox["max"], 4 * h + b + 1)
                    if h:
                        act.wait_ge(fox["tr"], 4 * (h - 1) + b + 1)
                    n = (b + 1) * P
                    nc.scalar.activation(tmp[:, b, 0:n], ps[:, b, 0:n], ACT.Exp, bias=negmax[:, 0, b:b + 1],
                                         accum_out=rowsum[:, 0, b:b + 1]).then_inc(fox["exp"], 1)

            def swa_exp(h):
                p = h % 2
                act.wait_ge(swa["max"], h + 1)
                nc.scalar.activation(sinkexp[:, p, :], negmax[:, p, :], ACT.Exp, bias=sink[:, h:h + 1])
                if h == 0:
                    act.wait_ge(fox["tr"], 4 * HEADS)
                elif h >= 2:
                    act.wait_ge(swa["tr"], 2 * (h - 1))
                for b in range(TB):
                    last = nc.scalar.activation(pb[:, p, b, :],
                                                ps[:, 2 * p + b // 2, 256 * (b % 2):256 * (b % 2) + 256], ACT.Exp,
                                                bias=negmax[:, p, b:b + 1], accum_out=rowsum[:, p, b:b + 1])
                last.then_inc(swa["exp"], 1)

            def run_mixer():
                for j in range(4):
                    split_hi(MIX + 4 + j)
                copy_factor(pre[1])
                for t in range(4):
                    high_part(t, h_hi[:, T_QA + t, :])
                for t in range(4):
                    split_hi(MIX + K_A + t + 4)
                    high_part(4 + t, h_hi[:, T_KA + t, :])
                split_hi(MIX + FG + 4)
                act.wait_ge(fgate, 3)
                nc.scalar.activation(tmp[0:HEADS, 1, :], tmp[0:HEADS, 1, :], ACT.Exp).then_inc(fgate_act, 1)
                act.wait_ge(fgate_act, 1)
                nc.scalar.activation(tmp[0:HEADS, 1, :], tmp[0:HEADS, 1, :], ACT.Ln, bias=1.0).then_inc(fgate_act, 1)
                act.wait_ge(fgate, 4)
                for r in (0, DH):
                    nc.scalar.activation(cum_r[r:r + HEADS, :], tmp[0:HEADS, 0, :], ACT.Copy,
                                         scale=-1.0).then_inc(fgate_act, 1)
                for t in range(4):
                    split_hi(MIX + Q_B + t + 4)
                    high_part(8 + t, h_hi[:, T_QB + t, :])
                split_hi(MIX + K_B + 4)
                high_part(12, h_hi[:, T_KB, :])
                for u in range(4):
                    split_hi(MIX + V_A + u + 4)
                for t in range(TB):
                    nc.scalar.activation(v_hi[:, t, 0:S], ps[:, V_BANKS[t], :], ACT.Copy,
                                         scale=rs[:, t:t + 1]).then_inc(v_hi_made, 1)
                split_hi(MIX + V_B + 4)
                for t in range(TB):
                    nc.scalar.activation(v_hi[:, t, S:S + P], ps[:, 3, t * P:(t + 1) * P], ACT.Copy,
                                         scale=rs[:, t:t + 1]).then_inc(v_hi_made, 1)

                def fox_high(h, blocks):
                    for b in blocks:
                        act.wait_ge(fox["tr"], 4 * h + b + 1)
                        if b == 0 and h:
                            act.wait_ge(fox["pv"], h)
                        nc.scalar.activation(pt_hi[:, 0:b + 1, b * P:(b + 1) * P],
                                             ps[:, 4 + b % 2, 0:(b + 1) * P].rearrange("p (j q) -> p j q", q=P),
                                             ACT.Copy).then_inc(fox["pth"], 1)

                split_hi(MIX + GATES + 4)
                fox_exp(0, range(TB))
                for h in range(HEADS):
                    if h + 1 < HEADS:
                        fox_high(h, (0, 1))
                        fox_exp(h + 1, (0, 1))
                        fox_high(h, (2,))
                        fox_exp(h + 1, (2,))
                        fox_high(h, (3,))
                        fox_exp(h + 1, (3,))
                    else:
                        fox_high(h, range(TB))
                        swa_exp(0)
                    split_hi(MIX + GATES + h + 5)
                    act.wait_ge(fox["pv"], h + 1)
                    r = DH * (h % 2)
                    nc.scalar.activation(h_hi[r:r + DH, T_QA + h // 2, :], ps[r:r + DH, 6, :],
                                         ACT.Copy).then_inc(fox["oh"], 1)
                for h in range(HEADS):
                    for g, n in ((0, 512), (1, 384)):
                        act.wait_ge(swa["tr"], 2 * h + g + 1)
                        if g == 0 and h >= 2:
                            act.wait_ge(swa["pv"], h - 1)
                        if g == 0 and h < 2:
                            act.wait_ge(fox["pv"], HEADS)
                        nc.scalar.activation(ptb_hi[:, h % 2, 512 * g:512 * g + n], ps[:, 4 + g, 0:n],
                                             ACT.Copy).then_inc(swa["pth"], 1)
                    if h + 1 < HEADS:
                        swa_exp(h + 1)
                    if h != HEADS - 2:
                        split_hi(MIX + GATES + HEADS + min(h, HEADS - 2) + 5)
                    act.wait_ge(swa["pv"], h + 1)
                    r = DH * (h % 2)
                    nc.scalar.activation(h_hi[r:r + DH, T_QB + h // 2, :], ps[r:r + DH, 6, :],
                                         ACT.Copy).then_inc(swa["oh"], 1)
                act.wait_ge(gate_evac, 2 * KD)
                with act.Fori(0, KD // 4) as i:
                    for j in range(4):
                        at = bass.ds(4 * i + j, 1)
                        for g in (x, gate_b):
                            v = g[:, at, :].rearrange("p a b -> p (a b)")
                            last = nc.scalar.activation(v, v, ACT.Sigmoid)
                        last.then_inc(gate_sig, 1)
                        split_hi(MIX + BRANCH + j + 4, i)
                        act.wait_ge(merged_val, 4 * i + (j + 1))
                        nc.scalar.activation(
                            h_hi[:, bass.ds(4 * i + (T_MERGED + j), 1), :].rearrange("p a b -> p (a b)"),
                            tmp[:, 2, :], ACT.Copy).then_inc(merged_hi, 1)
                with act.Fori(0, KD // 4) as i:
                    for j in range(4):
                        u0 = MIX + OUT + j
                        result_tile(j, 4 * i, j % 2, post[1], 3, 4 * i + (u0 + 1), mix_evac, u0 + 4, i)
                next_input(post[1], pre[2], 4)

            act.wait_ge(fills_made, 1)
            nc.scalar.activation(half[:, :], ones[:, 0:TB], ACT.Copy, scale=-0.5).then_inc(half_made, 1)
            act.wait_ge(gain_loaded, 16)
            for j, part in enumerate(X_PARTS):
                act.wait_ge(x_loaded[j], 16)
                for k in part:
                    high_input(k, pre[0], 0)
                if j == 0:
                    split_hi(FFN1)
                    split_hi(FFN1 + 1)
                for k in part:
                    square_input(k, pre[0])
            split_hi(FFN1 + 2)
            split_hi(FFN1 + 3)
            act.wait_ge(small_loaded, 64)
            nc.scalar.activation(ident_r[:, :], cst[:, 0:P], ACT.Copy)
            nc.scalar.activation(pick_r[:, :], cst[:, 4 * P:4 * P + HEADS], ACT.Copy)
            nc.scalar.activation(mask_r[:, :, :], cst[:, P:4 * P].rearrange("p (a b) -> p a b", a=3),
                                 ACT.Copy).then_inc(consts_split, 1)
            run_ffn(FFN1, ffn[0], pre[0], post[0], 1, pre[1], 2, MIX)
            run_mixer()
            run_ffn(FFN2, ffn[1], pre[2], post[2], 5, None, None, None)
            act.wait_ge(post[2]["bc"], 2)
            nc.scalar.activation(rsb[:, :], ps[:, 7, :], ACT.Copy).then_inc(last_factor, 1)

        @block.vector
        def _(dve):
            def split_lo(u0, i=0, elems=UNIT):
                s = u0 % RING
                dve.wait_ge(w_hi_made, RING * i + (u0 + 1))
                nc.vector.tensor_tensor(w_lo[:, s, 0:elems], raw[:, s, 0:elems], w_hi[:, s, 0:elems].bitcast(F32),
                                        ALU.subtract).then_inc(w_lo_made, 1)

            def low_input(k, n, g):
                dve.wait_ge(n["hi"], k + 1)
                nc.vector.scalar_tensor_tensor(xs_lo[:, k, :], x[:, k, :], gain[:, g, k:k + 1],
                                               xs_hi[:, k, :].bitcast(F32), ALU.mult, ALU.subtract).then_inc(n["lo"], 1)

            def mean_squares(n, bank, c):
                dve.wait_ge(n["ss"], 1)
                nc.vector.tensor_scalar(ms[:, :], ps[:, bank, 0:TB], c ** -2 / D, c ** -2 * EPS,
                                        ALU.mult, ALU.add).then_inc(n["ms"], 1)

            def diagonal(n):
                dve.wait_ge(n["rs"], 1)
                nc.vector.tensor_tensor(tmp[:, 3, :].rearrange("p (t q) -> p t q", t=TB),
                                        ident.unsqueeze(1).to_broadcast([P, TB, P]),
                                        rs[:, :].unsqueeze(2).to_broadcast([P, TB, P]), ALU.mult).then_inc(n["diag"], 1)

            def residual(n, evac, evacs, nnext, g, tiles):
                def scale(k):
                    nc.vector.tensor_tensor(y[:, k, :], ps[:, 5, :], y[:, k, :], ALU.mult).then_inc(n["t"], 1)

                dve.wait_ge(evac, evacs)
                dve.wait_ge(n["bc"], 1)
                if n is post[1]:
                    dve.wait_ge(x_back, 16 * KD)
                def add(k):
                    dve.wait_ge(n["t"], k + 1)
                    nc.vector.tensor_tensor(x[:, k, :], x[:, k, :], y[:, k, :], ALU.add).then_inc(n["x"], 1)

                scale(0)
                add(0)
                scale(1)
                if nnext is not None:
                    low_input(0, nnext, g)
                for k in range(1, tiles):
                    if k + 1 < tiles:
                        scale(k + 1)
                    add(k)
                    if nnext is not None and k > 1:
                        low_input(k - 1, nnext, g)
                if nnext is not None:
                    low_input(KD - 1, nnext, g)

            def run_ffn(base, f, npre, npost, nnext, gnext, next_base):
                nc.vector.memset(acc_post, 0.0).then_inc(npost["acc"], 1)
                for j in range(4):
                    split_lo(base + 4 + j)
                mean_squares(npre, 6, 1.0)
                diagonal(npre)
                dve.wait_ge(npre["rsb"], 1)

                def evacuate(t, i, bank):
                    dve.wait_ge(w_used, 2 * i + (base + 2 * t + 2))
                    nc.vector.tensor_tensor(tmp[:, 0, :], ps[:, bank, :], rsb[:, :], ALU.mult).then_inc(f["scaled"], 1)
                    nc.vector.tensor_tensor(tmp[:, 1, :], ps[:, bank + 1, :], rsb[:, :], ALU.mult).then_inc(f["evac"], 1)
                    dve.wait_ge(f["silu"], i + (t + 1))
                    dve.wait_ge(f["evac"], i + (t + 1))
                    nc.vector.tensor_tensor(tmp[:, 2, :], tmp[:, 0, :], tmp[:, 1, :], ALU.mult).then_inc(f["prod"], 1)
                    dve.wait_ge(f["hi"], i + (t + 1))
                    nc.vector.tensor_tensor(h_lo[:, bass.ds(i + t, 1), :].rearrange("p a b -> p (a b)"), tmp[:, 2, :],
                                            h_hi[:, bass.ds(i + t, 1), :].rearrange("p a b -> p (a b)").bitcast(F32),
                                            ALU.subtract).then_inc(f["lo"], 1)

                evacuate(0, 0, 0)
                evacuate(1, 0, 2)

                def tile(t, i, bank):
                    for j in range(2):
                        split_lo(base + 2 * t + 4 + j, i)
                    evacuate(t, 2 * i, bank)

                tile(2, 0, 4)
                tile(3, 0, 2)
                with dve.Fori(0, (KF - 6) // 2) as i:
                    tile(4, i, 0)
                    tile(5, i, 2)
                for t in (KF - 2, KF - 1):
                    for j in range(2):
                        c = 2 * (t - KF + 2) + j
                        split_lo(base + GATE_UP_UNITS + c, 0, DOWN_PARTS[c] * P)
                    evacuate(t, 0, 2 * (t % 2))

                def add_tile(d0, i):
                    dve.wait_ge(npost["sq"], i + (d0 + 1))
                    dve.wait_ge(npost["acc"], i + (d0 + 1))
                    nc.vector.tensor_tensor(acc_post, acc_post, sq[:, d0 % 2, :],
                                            ALU.add).then_inc(npost["acc"], 1)

                def down(d0, i, sizes, u0):
                    for c in range(3):
                        split_lo(u0 + c, i, sizes[c] * P)
                    add_tile(d0, i)
                    split_lo(u0 + 3, i, sizes[3] * P)

                u0 = base + GATE_UP_UNITS + 4
                with dve.Fori(0, (KD - 2) // 2) as i:
                    down(0, 2 * i, DOWN_PARTS, u0)
                    down(1, 2 * i, DOWN_PARTS, u0 + 4)
                down(KD - 2, 0, DOWN_PARTS, u0 + 4 * (KD - 2))
                if nnext is not None:
                    for c in range(RING - 1):
                        split_lo(next_base + c)
                mean_squares(npost, 2, 0.5)
                if nnext is not None:
                    split_lo(next_base + RING - 1)
                diagonal(npost)
                residual(npost, f["evac"], KF + KD, nnext, gnext, KD if nnext is not None else DVE_TILES)

            def scaled_tile(n, bank, scale, u):
                dve.wait_ge(w_used, MIX + u + 1)
                nc.vector.scalar_tensor_tensor(tmp[:, 2 + n % 2, :], ps[:, bank, :], scale, rsb[:, :], ALU.mult,
                                               ALU.mult).then_inc(proj_evac, 1)

            def low_part(n, dst_hi, dst_lo):
                dve.wait_ge(proj_hi, n + 1)
                nc.vector.tensor_tensor(dst_lo, tmp[:, 2 + n % 2, :], dst_hi.bitcast(F32), ALU.subtract).then_inc(proj_lo, 1)

            def roped_tile(n, bank, scale, u):
                dve.wait_ge(w_used, MIX + u + 1)
                nc.vector.scalar_tensor_tensor(tmp[:, 0, :], ps[:, bank, :], scale, cos, ALU.mult, ALU.mult)
                for a in range(4):
                    r, o = 32 * a, 32 * (a ^ 1)
                    last = nc.vector.scalar_tensor_tensor(tmp[o:o + 32, 1, :], ps[r:r + 32, bank, :], scale,
                                                          sin[r:r + 32, :], ALU.mult, ALU.mult)
                last.then_inc(proj_evac, 1)
                dve.wait_ge(proj_evac, n + 2)
                nc.vector.tensor_tensor(tmp[:, 2 + n % 2, :], tmp[:, 0, :], tmp[:, 1, :], ALU.add).then_inc(proj_val, 1)

            def fox_max(h, blocks):
                for b in blocks:
                    dve.wait_ge(fox["score"], 4 * h + b + 1)
                    nc.vector.tensor_reduce(negmax[:, 0, b:b + 1], ps[:, b, 0:(b + 1) * P], AX.X, ALU.max,
                                            negate=True).then_inc(fox["max"], 1)

            def fox_recip(h, blocks):
                for b in blocks:
                    dve.wait_ge(fox["exp"], 4 * h + b + 1)
                    nc.vector.reciprocal(recip[:, 0, b:b + 1], rowsum[:, 0, b:b + 1]).then_inc(fox["rec"], 1)

            def swa_max(h):
                p = h % 2
                dve.wait_ge(swa["score"], h + 1)
                nc.vector.tensor_reduce(negmax[:, p, :],
                                        ps[:, 2 * p:2 * p + 2, :].rearrange("p a (b c) -> p (a b) c", b=2),
                                        AX.X, ALU.max, negate=True).then_inc(swa["rawmax"], 1)
                dve.wait_ge(swa["rawmax"], h + 1)
                nc.vector.tensor_scalar(negmax[:, p, :], negmax[:, p, :], nsink[:, h:h + 1], None,
                                        ALU.min).then_inc(swa["max"], 1)

            def swa_recip(h):
                p = h % 2
                dve.wait_ge(swa["exp"], h + 1)
                nc.vector.tensor_tensor(rowsum[:, p, :], rowsum[:, p, :], sinkexp[:, p, :], ALU.add).then_inc(swa["sum"], 1)
                dve.wait_ge(swa["sum"], h + 1)
                nc.vector.reciprocal(recip[:, p, :], rowsum[:, p, :]).then_inc(swa["rec"], 1)

            def run_mixer():
                npre = pre[1]
                for j in range(4):
                    split_lo(MIX + 4 + j)
                mean_squares(npre, 6, 1.0)
                diagonal(npre)
                dve.wait_ge(npre["rsb"], 1)
                for n in range(4):
                    scaled_tile(n, n, SCALE, Q_A + n)
                    low_part(n, h_hi[:, T_QA + n, :], h_lo[:, T_QA + n, :])
                nc.vector.tensor_tensor(cos, cos, rsb[:, :], ALU.mult)
                nc.vector.tensor_tensor(sin, sin, rsb[:, :], ALU.mult).then_inc(rope_scaled, 1)
                for t in range(4):
                    n = 4 + t
                    split_lo(MIX + K_A + t + 4)
                    scaled_tile(n, (4, 5, 0, 1)[t], 1.0, K_A + t)
                    low_part(n, h_hi[:, T_KA + t, :], h_lo[:, T_KA + t, :])
                split_lo(MIX + FG + 4)
                dve.wait_ge(w_used, MIX + FG + 1)
                z, a, zero = tmp[0:HEADS, 0, :], tmp[0:HEADS, 1, :], tmp[0:HEADS, 2, :]
                nc.vector.memset(zero, 0.0)
                nc.vector.tensor_tensor(z, ps[0:HEADS, 6, :], rsb[0:HEADS, :], ALU.mult).then_inc(proj_evac, 1)
                dve.wait_ge(proj_evac, 9)
                nc.vector.tensor_scalar(z, z, fbias[:, 0:1], None, ALU.add).then_inc(fgate, 2)
                dve.wait_ge(fgate, 2)
                nc.vector.scalar_tensor_tensor(a, z, -1.0, z, ALU.mult, ALU.min).then_inc(fgate, 1)
                dve.wait_ge(fgate_act, 2)
                nc.vector.scalar_tensor_tensor(a, z, 0.0, a, ALU.min, ALU.subtract).then_inc(rope_parts, 1)
                dve.wait_ge(rope_parts, 1)
                nc.vector.tensor_tensor_scan(z, a, zero, 0.0, ALU.add, ALU.add).then_inc(fgate, 1)
                dve.wait_ge(fgate_act, 4)
                for r in (0, DH):
                    last = nc.vector.scalar_tensor_tensor(cum_r[r + 32:r + 32 + HEADS, :], z, -1.0,
                                                          cum_r[0:HEADS, :].bitcast(F32), ALU.mult, ALU.subtract)
                last.then_inc(fgate, 1)
                dve.wait_ge(rope_scaled, 1)
                dve.wait_ge(fgate, 5)
                for t in range(4):
                    split_lo(MIX + Q_B + t + 4)
                    roped_tile(8 + t, (2, 3, 0, 1)[t], SCALE, Q_B + t)
                    low_part(8 + t, h_hi[:, T_QB + t, :], h_lo[:, T_QB + t, :])
                split_lo(MIX + K_B + 4)
                roped_tile(12, 7, 1.0, K_B)
                low_part(12, h_hi[:, T_KB, :], h_lo[:, T_KB, :])
                for u in range(4):
                    split_lo(MIX + V_A + u + 4)
                for t in range(TB):
                    dve.wait_ge(v_hi_made, t + 1)
                    nc.vector.scalar_tensor_tensor(v_lo[:, t, 0:S], ps[:, V_BANKS[t], :], rs[:, t:t + 1],
                                                   v_hi[:, t, 0:S].bitcast(F32), ALU.mult,
                                                   ALU.subtract).then_inc(proj_evac, 1)
                split_lo(MIX + V_B + 4)
                dve.wait_ge(v_hi_made, 2 * TB)
                for t in range(TB):
                    last = nc.vector.scalar_tensor_tensor(v_lo[:, t, S:S + P], ps[:, 3, t * P:(t + 1) * P],
                                                          rs[:, t:t + 1], v_hi[:, t, S:S + P].bitcast(F32),
                                                          ALU.mult, ALU.subtract)
                last.then_inc(proj_evac, 1)

                def fox_low(h, blocks):
                    for b in blocks:
                        dve.wait_ge(fox["pth"], 4 * h + b + 1)
                        nc.vector.tensor_tensor(pt_lo[:, 0:b + 1, b * P:(b + 1) * P],
                                                ps[:, 4 + b % 2, 0:(b + 1) * P].rearrange("p (j q) -> p j q", q=P),
                                                pt_hi[:, 0:b + 1, b * P:(b + 1) * P].bitcast(F32),
                                                ALU.subtract).then_inc(fox["ptl"], 1)

                def gate_out(v):
                    dve.wait_ge(w_used, MIX + GATES + v + 1)
                    nc.vector.tensor_tensor((x, gate_b)[v % 2][:, v // 2, :], ps[:, 7, :], rsb[:, :],
                                            ALU.mult).then_inc(gate_evac, 1)

                dve.wait_ge(x_saved, 16)
                gate_out(0)
                split_lo(MIX + GATES + 4)
                fox_max(0, range(TB))
                fox_recip(0, range(TB))
                for h in range(HEADS):
                    gate_out(h + 1)
                    if h + 1 < HEADS:
                        fox_low(h, (0, 1))
                        fox_max(h + 1, (0, 1))
                        fox_recip(h + 1, (0, 1))
                        fox_low(h, (2,))
                        fox_max(h + 1, (2,))
                        fox_low(h, (3,))
                        fox_max(h + 1, (3,))
                        fox_recip(h + 1, (2, 3))
                    else:
                        fox_low(h, range(TB))
                        swa_max(0)
                        swa_recip(0)
                    split_lo(MIX + GATES + h + 5)
                    dve.wait_ge(fox["oh"], h + 1)
                    r = DH * (h % 2)
                    nc.vector.tensor_tensor(h_lo[r:r + DH, T_QA + h // 2, :], ps[r:r + DH, 6, :],
                                            h_hi[r:r + DH, T_QA + h // 2, :].bitcast(F32),
                                            ALU.subtract).then_inc(fox["ol"], 1)
                for h in range(HEADS):
                    if h != HEADS - 2:
                        gate_out(HEADS + min(h, HEADS - 2) + 1)
                    if h + 1 < HEADS:
                        swa_max(h + 1)
                    for g, n in ((0, 512), (1, 384)):
                        dve.wait_ge(swa["pth"], 2 * h + g + 1)
                        nc.vector.tensor_tensor(ptb_lo[:, h % 2, 512 * g:512 * g + n], ps[:, 4 + g, 0:n],
                                                ptb_hi[:, h % 2, 512 * g:512 * g + n].bitcast(F32),
                                                ALU.subtract).then_inc(swa["ptl"], 1)
                    if h + 1 < HEADS:
                        swa_recip(h + 1)
                    if h != HEADS - 2:
                        split_lo(MIX + GATES + HEADS + min(h, HEADS - 2) + 5)
                    dve.wait_ge(swa["oh"], h + 1)
                    r = DH * (h % 2)
                    nc.vector.tensor_tensor(h_lo[r:r + DH, T_QB + h // 2, :], ps[r:r + DH, 6, :],
                                            h_hi[r:r + DH, T_QB + h // 2, :].bitcast(F32),
                                            ALU.subtract).then_inc(mix_evac, 1)

                with dve.Fori(0, KD // 4) as i:
                    for j in range(4):
                        b = 2 * (j % 2)
                        dve.wait_ge(w_used, 4 * i + (MIX + BRANCH + j + 1))
                        dve.wait_ge(gate_sig, 4 * i + (j + 1))
                        at = bass.ds(4 * i + j, 1)
                        nc.vector.tensor_tensor(tmp[:, 0, :], ps[:, b, :], x[:, at, :].rearrange("p a b -> p (a b)"),
                                                ALU.mult).then_inc(branch_parts, 1)
                        nc.vector.tensor_tensor(tmp[:, 1, :], ps[:, b + 1, :],
                                                gate_b[:, at, :].rearrange("p a b -> p (a b)"),
                                                ALU.mult).then_inc(mix_evac, 1)
                        dve.wait_ge(mix_evac, 4 * i + (HEADS + j + 1))
                        nc.vector.tensor_tensor(tmp[:, 2, :], tmp[:, 0, :], tmp[:, 1, :], ALU.add).then_inc(merged_val, 1)
                        split_lo(MIX + BRANCH + j + 4, i)
                        dve.wait_ge(merged_hi, 4 * i + (j + 1))
                        at = bass.ds(4 * i + (T_MERGED + j), 1)
                        nc.vector.tensor_tensor(h_lo[:, at, :].rearrange("p a b -> p (a b)"), tmp[:, 2, :],
                                                h_hi[:, at, :].rearrange("p a b -> p (a b)").bitcast(F32),
                                                ALU.subtract).then_inc(merged_lo, 1)
                nc.vector.memset(acc_post, 0.0).then_inc(post[1]["acc"], 1)
                for j in range(KD):
                    if j < KD - 1:
                        dve.wait_ge(post[1]["sq"], j + 1)
                        dve.wait_ge(post[1]["acc"], j + 1)
                        nc.vector.tensor_tensor(acc_post, acc_post, sq[:, j % 2, :], ALU.add).then_inc(post[1]["acc"], 1)
                        split_lo(MIX + OUT + j + 4)
                mean_squares(post[1], 2, 1.0)
                split_lo(FFN2 + RING - 1)
                diagonal(post[1])
                residual(post[1], mix_evac, HEADS + 2 * KD, pre[2], 4, KD)

            nc.vector.memset(ones[:, :], 1.0).then_inc(fills_made, 1)
            nc.vector.memset(cum_r[:, :].bitcast(F32), 0.0).then_inc(fills_made, 1)
            for k in range(KD):
                low_input(k, pre[0], 0)
                if k == 0:
                    split_lo(FFN1)
                    split_lo(FFN1 + 1)
            split_lo(FFN1 + 2)
            split_lo(FFN1 + 3)
            dve.wait_ge(small_loaded, 64)
            nc.vector.tensor_scalar(nsink[:, :], sink[:, :], -1.0, None, ALU.mult)
            run_ffn(FFN1, ffn[0], pre[0], post[0], pre[1], 2, MIX)
            run_mixer()
            run_ffn(FFN2, ffn[1], pre[2], post[2], None, None, None)

        @block.gpsimd
        def _(pool):
            def pre_squares(n):
                nc.gpsimd.memset(acc_pre, 0.0).then_inc(n["acc"], 1)
                for k in range(KD):
                    pool.wait_ge(n["sq"], k + 1)
                    pool.wait_ge(n["acc"], k + 1)
                    nc.gpsimd.tensor_tensor(acc_pre, acc_pre, sq[:, k % 2, :], ALU.add).then_inc(n["acc"], 1)

            def last_tiles(n):
                for k in range(DVE_TILES, KD):
                    pool.wait_ge(ffn[1]["evac"], KF + k + 1)
                    pool.wait_ge(last_factor, 1)
                    nc.gpsimd.tensor_tensor(y[:, k, :], rsb[:, :], y[:, k, :], ALU.mult).then_inc(pool_scaled, 1)
                    pool.wait_ge(pool_scaled, k - DVE_TILES + 1)
                    nc.gpsimd.tensor_tensor(x[:, k, :], x[:, k, :], y[:, k, :], ALU.add).then_inc(pool_summed, 1)

            def power(n):
                pool.wait_ge(n["ms"], 1)
                nc.gpsimd.tensor_tensor(rs[:, :], ms[:, :], half[:, :], ALU.pow).then_inc(n["rs"], 1)

            pool.wait_ge(half_made, 1)
            pre_squares(pre[0])
            power(pre[0])
            power(post[0])
            pre_squares(pre[1])
            power(pre[1])
            for h in range(HEADS):
                for b in range(TB):
                    pool.wait_ge(fox["rec"], 4 * h + b + 1)
                    n = (b + 1) * P
                    nc.gpsimd.tensor_scalar(tmp[:, b, 0:n], tmp[:, b, 0:n], recip[:, 0, b:b + 1], None,
                                            ALU.mult).then_inc(fox["norm"], 1)
            for h in range(HEADS):
                pool.wait_ge(swa["rec"], h + 1)
                nc.gpsimd.tensor_tensor(pb[:, h % 2], pb[:, h % 2],
                                        recip[:, h % 2, :].unsqueeze(2).to_broadcast([P, TB, 2 * P]),
                                        ALU.mult).then_inc(swa["norm"], 1)
            power(post[1])
            pre_squares(pre[2])
            power(pre[2])
            power(post[2])
            last_tiles(post[2])


def tiles(w, rows):
    return w.reshape(rows, P, -1, P).transpose(2, 1, 0, 3).reshape(-1, P, rows * P)


def kernel(**inputs):
    import concourse.bacc as _bacc
    from concourse.bass_utils import run_bass_kernel_spmd as _run

    a = {k: np.asarray(v) for k, v in inputs.items()}

    def gate_up(n):
        g, u = tiles(a[f"ffn{n}_w_gate"][0], KD), tiles(a[f"ffn{n}_w_up"][0], KD)
        return np.ascontiguousarray(np.stack([g, u], axis=1).reshape(-1, P, UNIT))

    w_in = a["w_in"][0]
    fox = HEADS * DH
    cuts = np.cumsum([0, fox, fox, fox, HEADS, fox, P, P, D, D])
    q_a, k_a, v_a, f_a, q_b, k_b, v_b, gate_a, gate_b = (w_in[:, s:e] for s, e in zip(cuts[:-1], cuts[1:]))
    order = np.arange(HEADS).reshape(2, HEADS // 2).T.reshape(-1)
    q_b = q_b.reshape(D, HEADS, DH)[:, order].reshape(D, fox)
    w_swa = a["w_branch_swa"][0].reshape(HEADS, DH, D)[order].reshape(fox, D)
    f_wide = w_in[:, cuts[3]:cuts[3] + P]
    v_units = v_a.reshape(4, 2, P, fox).transpose(0, 2, 1, 3).reshape(4, P, UNIT)
    branch = np.concatenate([tiles(a["w_branch_fox"][0], 4), tiles(w_swa, 4)], axis=2)
    gates = np.stack([tiles(gate_a, KD), tiles(gate_b, KD)], axis=1).reshape(-1, P, UNIT)
    mixw = np.concatenate([tiles(q_a, KD), tiles(k_a, KD), tiles(f_wide, KD), tiles(q_b, KD), tiles(k_b, KD),
                           v_units, tiles(v_b, KD), gates, branch, tiles(a["w_out"][0], KD)], axis=0)

    gains = np.stack([a[n][0].reshape(KD, P).T for n in ("ffn1_pre_g", "ffn1_post_g", "mix_pre_g", "mix_post_g",
                                                         "ffn2_pre_g", "ffn2_post_g")], axis=1)
    sinks = np.broadcast_to(a["swa_sinks"][0][order], (P, HEADS))

    i = np.arange(P)
    before = np.where(i[None, :] > i[:, None], 0.0, MASKED)
    same = np.where(i[None, :] <= i[:, None], 0.0, MASKED)
    pick = ((i[:, None] % 32 == np.arange(HEADS)[None, :]) & (i[:, None] % DH < 40)).astype(np.float32)
    consts = np.concatenate([np.eye(P), before, same, np.full((P, P), MASKED), pick], axis=1).astype(np.float32)
    inv = (np.float32(1.0) / np.float32(10000.0) ** (np.arange(0, DH, 2, dtype=np.float32) / np.float32(DH)))
    ang = (np.arange(S, dtype=np.float32)[:, None] * inv.astype(np.float32)[None, :]).T
    cos, sin = np.cos(ang), np.sin(ang)
    rope = np.stack([np.tile(cos, (4, 1)), np.tile(np.concatenate([sin, -sin]), (2, 1))], axis=1).astype(np.float32)

    arrays = {
        "x_in": a["x"][0].T.reshape(KD, P, S).transpose(1, 0, 2),
        "gu1": gate_up(1), "dn1": tiles(a["ffn1_w_down"][0], KF), "mixw": mixw,
        "gu2": gate_up(2), "dn2": tiles(a["ffn2_w_down"][0], KF), "gains": gains, "sinks": sinks,
        "forget_bias": a["fox_forget_bias"][0].reshape(HEADS, 1), "consts": consts, "rope": rope,
    }
    arrays = {k: np.ascontiguousarray(v) for k, v in arrays.items()}

    nc = _bacc.Bacc("TRN2", target_bir_lowering=False, num_devices=1, dynamic_dma_scratch_size=1024)
    args = [nc.dram_tensor(k, v.shape, F32, kind="ExternalInput").ap() for k, v in arrays.items()]
    x_kept = nc.dram_tensor("x_kept", (P, KD, S), F32).ap()
    out = nc.dram_tensor("out", (P, KD, S), F32, kind="ExternalOutput").ap()
    build(nc, *args, x_kept, out)
    r = _run(nc, [arrays], core_ids=[0])
    got = np.asarray(r.results[0]["out"])
    return np.ascontiguousarray(got.transpose(1, 0, 2).reshape(D, S).T)[None]
```

```python
from contextlib import ExitStack

import numpy as np
import concourse.bass as bass
from concourse import mybir

F32 = mybir.dt.float32
F32R = mybir.dt.float32r
ACT = mybir.ActivationFunctionType
ALU = mybir.AluOpType
AX = mybir.AxisListType

P = 128
D = 1024
S = 512
F = 2816
DH = 64
HEADS = 8
KD = D // P
KF = F // P
TB = S // P
EPS = 1e-6
SCALE = DH ** -0.5
MASKED = -(2.0 ** 126)

HALF = S // 2
LAST_BANKS = (1, 4)
SUM_BANKS = (2, 7)
FACTOR_BANKS = (5, 6)
DVE_TILES = 6
COPY_BANK = 3

WARM_UP = 15

RING = 4
UNIT = 8 * P
DOWN_PARTS = (6, 5, 6, 5)
DOWN_FROM = (0, 6, 11, 17)

X_PARTS = ((0,), (1,), (2, 3), (4, 5), (6, 7))

GATE_UP_UNITS = 2 * KF
DOWN_UNITS = 4 * KD
FFN_UNITS = GATE_UP_UNITS + DOWN_UNITS
Q_A, K_A, FG, Q_B, K_B, V_A, V_B = 0, 4, 8, 9, 13, 14, 18
GATES = 19
BRANCH = GATES + 2 * KD
OUT = BRANCH + KD
MIX_UNITS = OUT + KD
FFN1, MIX, FFN2 = 0, FFN_UNITS, FFN_UNITS + MIX_UNITS

T_QA, T_QB, T_KA, T_KB, T_V, T_PT = 0, 4, 8, 12, 13, 18
T_MERGED = 8
V_BANKS = (4, 5, 6, 2)


def build(nc, x_in, gu1, dn1, mixw, gu2, dn2, gains, sinks, forget_bias, consts, rope, x_kept, out):
    with ExitStack() as ctx:
        def sb(name, shape, dt=F32):
            return ctx.enter_context(nc.sbuf_tensor(name, shape, dt))

        def sem(name):
            return ctx.enter_context(nc.semaphore(name))

        xs_hi = sb("xs_hi", [P, KD, S], F32R)
        xs_lo_at = -(-nc.sbuf_base // 32) * 32
        xs_lo = sb("xs_lo", [P, KD, S], F32R)
        h_hi = sb("h_hi", [P, KF, S], F32R)
        h_lo = sb("h_lo", [P, KF, S], F32R)
        w_hi = sb("w_hi", [P, RING, UNIT], F32R)
        w_lo = sb("w_lo", [P, RING, UNIT], F32R)
        ident_r = sb("ident_r", [P, P], F32R)
        mask_r = sb("mask_r", [P, 3, P], F32R)
        pick_r = sb("pick_r", [P, HEADS], F32R)
        cum_r = sb("cum_r", [P, S], F32R)
        x = sb("x", [P, KD, S])
        raw = sb("raw", [P, RING, UNIT])
        tmp = sb("tmp", [P, 4, S])
        gate_b = sb("gate_b", [P, KD, S])
        rsb = sb("rsb", [P, S])
        cst = sb("cst", [P, 4 * P + HEADS])
        ones = sb("ones", [P, P])
        gain = sb("gain", [P, 6, KD])
        sink = sb("sink", [P, HEADS])
        nsink = sb("nsink", [P, HEADS])
        fbias = sb("fbias", [HEADS, 1])
        ms = sb("ms", [P, TB])
        rs = sb("rs", [P, TB])
        half = sb("half", [P, TB])
        negmax = sb("negmax", [P, 2, TB])
        rowsum = sb("rowsum", [P, 2, TB])
        sinkexp = sb("sinkexp", [P, 2, TB])
        recip = sb("recip", [P, 2, TB])
        y = nc.alloc_sbuf_tensor_at("y", [P, KD, S], F32, offset=xs_lo_at)
        ps = ctx.enter_context(nc.psum_tensor("ps", [P, 8, S], F32))

        ident = cst[:, 0:P]
        ropes = gate_b[:, 0:2, :]
        cos, sin = gate_b[:, 0, :], gate_b[:, 1, :]
        sq, acc_pre, acc_post = gate_b[:, 4:6, :], gate_b[:, 6, :], gate_b[:, 7, :]
        v_pairs = [h[:, T_V:T_V + 5, :].rearrange("p a b -> p (a b)").rearrange("p (t c) -> p t c", t=2)
                   for h in (h_hi, h_lo)]

        def v_head(t, h):
            return v_pairs[t // 2][:, t % 2, P * h:P * (h + 1)]

        def v_part(t, e):
            return v_pairs[t // 2][:, t % 2, 0:P * HEADS].rearrange("p (h e c) -> p h e c", e=2, c=DH)[:, :, e, :]

        def v_kv_part(half, n, e):
            a = P * (HEADS + n) + DH * e
            return v_pairs[half][:, :, a:a + DH]

        pt_hi, pt_lo = h_hi[:, T_PT:T_PT + 4, :], h_lo[:, T_PT:T_PT + 4, :]
        ptb_hi = pt_hi.rearrange("p a b -> p (a b)").rearrange("p (u c) -> p u c", u=2)
        ptb_lo = pt_lo.rearrange("p a b -> p (a b)").rearrange("p (u c) -> p u c", u=2)
        pb = tmp[:, :, :].rearrange("p a b -> p (a b)").rearrange("p (u b c) -> p u b c", u=2, b=TB)

        w_loaded = [sem(f"w_loaded{i}") for i in range(RING)]
        w_hi_made = sem("w_hi_made")
        w_lo_made = sem("w_lo_made")
        w_used = sem("w_used")
        small_loaded = sem("small_loaded")
        gain_loaded = sem("gain_loaded")
        x_loaded = [sem(f"x_loaded{i}") for i in range(len(X_PARTS))]
        fills_made = sem("fills_made")
        half_made = sem("half_made")
        consts_split = sem("consts_split")
        pre = [{n: sem(f"pre{i}_{n}") for n in ("hi", "lo", "sq", "acc", "ss", "ms", "rs", "diag", "bc", "rsb")}
               for i in range(3)]
        post = [{n: sem(f"post{i}_{n}") for n in ("half", "sq", "acc", "ss", "ms", "rs", "diag", "bc", "t", "x")}
                for i in range(3)]
        ffn = [{n: sem(f"ffn{i}_{n}") for n in ("scaled", "silu", "prod", "hi", "lo", "evac")} for i in range(2)]
        proj_evac = sem("proj_evac")
        proj_val = sem("proj_val")
        proj_hi = sem("proj_hi")
        proj_lo = sem("proj_lo")
        v_hi_made = sem("v_hi_made")
        rope_scaled = sem("rope_scaled")
        fgate_negative = sem("fgate_negative")
        swa_v_turned = sem("swa_v_turned")
        fgate = sem("fgate")
        fgate_act = sem("fgate_act")
        fox = {n: sem(f"fox_{n}") for n in ("score", "max", "exp", "rec", "norm", "tr", "pth", "ptl", "pv", "ocopy", "osum", "oh", "ol")}
        swa = {n: sem(f"swa_{n}") for n in ("score", "rawmax", "max", "exp", "sum", "rec", "norm", "tr", "pth", "ptl",
                                            "pv", "ocopy", "osum", "oh")}
        mix_evac = sem("mix_evac")
        x_saved = sem("x_saved")
        x_back = sem("x_back")
        gate_evac = sem("gate_evac")
        gate_sig = sem("gate_sig")
        merged_val = sem("merged_val")
        merged_hi = sem("merged_hi")
        merged_lo = sem("merged_lo")
        last_factor_out = sem("last_factor_out")
        last_factor = sem("last_factor")
        pool_scaled = sem("pool_scaled")
        pool_summed = sem("pool_summed")
        stored = sem("stored")

        def turned(i, n):
            return ps[:, 5, :].rearrange("p (t c) -> p t c", t=TB)[:, 2 * i:2 * i + 2, DH * n:DH * (n + 1)]

        def head_sum(t0, h):
            o = tmp[:, 0, :] if t0 == T_QB and h == HEADS - 1 else gate_b[:, KD - 1, :]
            return o[DH * (h % 2):DH * (h % 2) + DH, :]

        def head_out(tensor, t0, h):
            return tensor[DH * (h % 2):DH * (h % 2) + DH, t0 + h // 2, :]

        block = ctx.enter_context(nc.Block())

        def loads_of(u0):
            return u0 % RING, 16 * (u0 // RING + 1)

        @block.sync
        def _(sp):
            def load(u0, i, src, elems):
                if not (isinstance(i, int) and u0 + RING * i < RING):
                    sp.wait_ge(w_lo_made, RING * i + (u0 - RING + 1))
                sp.dma_start(raw[:, u0 % RING, 0:elems], src).then_inc(w_loaded[u0 % RING], 16)

            def ffn_loads(base, gu, dn, first):
                def x_load(j):
                    a, b = X_PARTS[j][0], X_PARTS[j][-1] + 1
                    sp.dma_start(x[:, a:b, :], x_in[:, a:b, :]).then_inc(x_loaded[j], 16)

                if first:
                    x_load(0)
                load(base, 0, gu[0], UNIT)
                load(base + 1, 0, gu[1], UNIT)
                if first:
                    for j in range(1, len(X_PARTS)):
                        x_load(j)
                load(base + 2, 0, gu[2], UNIT)
                load(base + 3, 0, gu[3], UNIT)
                if first:
                    sp.dma_start(cst[:, :], consts).then_inc(small_loaded, 16)
                    sp.dma_start(ropes, rope).then_inc(small_loaded, 16)
                    sp.dma_start(sink[:, :], sinks).then_inc(small_loaded, 16)
                    sp.dma_start(fbias[:, :], forget_bias).then_inc(small_loaded, 16)
                with sp.Fori(1, GATE_UP_UNITS // RING) as i:
                    for j in range(RING):
                        load(base + j, i, gu[bass.ds(RING * i + j, 1)].rearrange("a p n -> (a p) n"), UNIT)
                with sp.Fori(0, KD) as d:
                    for c in range(4):
                        n, at = DOWN_PARTS[c] * P, DOWN_FROM[c] * P
                        load(base + GATE_UP_UNITS + c, d,
                             dn[bass.ds(d, 1), :, at:at + n].rearrange("a p n -> (a p) n"), n)

            sp.dma_start(gain[:, :, :], gains).then_inc(gain_loaded, 16)
            ffn_loads(FFN1, gu1, dn1, True)
            for u in range(2 * RING):
                load(MIX + u, 0, mixw[u], UNIT)
            sp.wait_ge(post[0]["x"], 2 * KD)
            sp.dma_start(x_kept, x[:, :, :]).then_inc(x_saved, 16)
            with sp.Fori(0, (OUT - 2 * RING) // RING) as i:
                for j in range(RING):
                    u = 2 * RING + j
                    load(MIX + u, i, mixw[bass.ds(RING * i + u, 1)].rearrange("a p n -> (a p) n"), UNIT)
            for u in range(OUT // RING * RING, OUT):
                load(MIX + u, 0, mixw[u], UNIT)
            sp.wait_ge(x_saved, 16)
            for k in range(KD):
                load(MIX + OUT + k, 0, mixw[OUT + k], UNIT)
                sp.wait_ge(merged_val, k + 1)
                sp.dma_start(x[:, k, :], x_kept[:, k, :]).then_inc(x_back, 16)
            ffn_loads(FFN2, gu2, dn2, False)
            for h in range(2):
                for a, b in (((0, 3), (3, 6), (6, 8)), ((0, 2), (2, 4), (6, 7), (4, 6), (7, 8)))[h]:
                    if h == 0 or b <= DVE_TILES:
                        sp.wait_ge(post[2]["x"], h * KD + b)
                    else:
                        sp.wait_ge(pool_summed, b - DVE_TILES)
                    sp.dma_start(out[:, a:b, h * HALF:(h + 1) * HALF],
                                 x[:, a:b, h * HALF:(h + 1) * HALF]).then_inc(stored, 16)
            sp.wait_ge(stored, 16 * 8)

        @block.tensor
        def _(pe):
            def product(o, st, mv, first=False, last=False):
                nc.tensor.matmul(o, st[0], mv[0], start=first, stop=False, skip_group_check=True)
                nc.tensor.matmul(o, st[0], mv[1], start=False, stop=False, skip_group_check=True)
                return nc.tensor.matmul(o, st[1], mv[0], start=False, stop=last, skip_group_check=True)

            def wblock(u0, k, width=P):
                s = u0 % RING
                return w_hi[:, s, k * width:(k + 1) * width], w_lo[:, s, k * width:(k + 1) * width]

            def xtile(k, a=0, b=S):
                return xs_hi[:, k, a:b], xs_lo[:, k, a:b]

            def htile(k, a=0, b=S):
                return h_hi[:, k, a:b], h_lo[:, k, a:b]

            def sum_squares(n):
                pe.wait_ge(n["acc"], KD + 1)
                for t in range(TB):
                    last = nc.tensor.matmul(ps[:, 6, t:t + 1], acc_pre[:, t * P:(t + 1) * P], ones[:, 0:1],
                                            start=True, stop=True)
                last.then_inc(n["ss"], 1)

            def sum_result_squares(n, h):
                pe.wait_ge(n["acc"], KD)
                pe.wait_ge(n["sq"], KD + h)
                for t in (2 * h, 2 * h + 1):
                    o = ps[:, SUM_BANKS[h], t:t + 1]
                    nc.tensor.matmul(o, acc_post[:, t * P:(t + 1) * P], ones[:, 0:1],
                                     start=(t == 2 * h), stop=False, skip_group_check=True)
                    last = nc.tensor.matmul(o, sq[:, 1, t * P:(t + 1) * P], ones[:, 0:1],
                                            start=False, stop=True, skip_group_check=True)
                last.then_inc(n["ss"], 1)

            def broadcast_factor(n, bank):
                pe.wait_ge(n["diag"], 1)
                nc.tensor.matmul(ps[:, bank, :], ones[:, :], tmp[:, 3, :], start=True, stop=True).then_inc(n["bc"], 1)

            def broadcast_half(n, h, bank, done):
                pe.wait_ge(n["diag"], h + 1)
                a, b = h * HALF, (h + 1) * HALF
                nc.tensor.matmul(ps[:, bank, a:b], ones[:, :], tmp[:, 3, a:b], start=True, stop=True).then_inc(done, 1)

            def last_tile(n, parts, tile_of):
                total = sum(blocks for _, _, blocks in parts)
                for h in range(2):
                    t = 0
                    for c, (u0, k0, blocks) in enumerate(parts):
                        if h == 0:
                            pe.wait_ge(w_lo_made, u0 + 1)
                        for k in range(k0, k0 + blocks):
                            last = product(ps[:, LAST_BANKS[h], h * HALF:(h + 1) * HALF], wblock(u0, k),
                                           tile_of(t, h * HALF, (h + 1) * HALF), first=(t == 0), last=(t == total - 1))
                            t += 1
                        if h == 1:
                            if c + 1 == len(parts) or parts[c + 1][0] != u0:
                                last.then_inc(w_used, 1)
                            if c == 0:
                                sum_result_squares(n, 0)
                            if c == 1 and len(parts) == 4:
                                broadcast_half(n, 0, FACTOR_BANKS[0], n["bc"])
                    if h == 0:
                        last.then_inc(n["half"], 1)

            def first_group(base, n, width):
                for k in range(KD // 2):
                    pe.wait_ge(n["lo"], k + 1)
                    for j in range(width):
                        if k == 0:
                            pe.wait_ge(w_lo_made, base + j + 1)
                        product(ps[:, j, :], wblock(base + j, k), xtile(k), first=(k == 0))
                for j in range(width):
                    for k in range(KD // 2, KD):
                        if j == 0:
                            pe.wait_ge(n["lo"], k + 1)
                        last = product(ps[:, j, :], wblock(base + j, k), xtile(k), last=(k == KD - 1))
                    last.then_inc(w_used, 1)

            def first_group_halves(base, n, nlast):
                def block(j, k, h):
                    if k == 0 and h == 0:
                        pe.wait_ge(w_lo_made, base + j + 1)
                    a, b = h * HALF, (h + 1) * HALF
                    return product(ps[:, j, a:b], wblock(base + j, k), xtile(k, a, b), first=(k == 0 and h == 0),
                                   last=(k == KD - 1))

                for k in range(KD):
                    pe.wait_ge(n["lo"], k + 1)
                    for j in range(2):
                        block(j, k, 0)
                    for j, joins in ((2, 1), (3, 3)):
                        for i in (() if k < joins else range(k + 1) if k == joins else (k,)):
                            block(j, i, 0)
                    if k == 0:
                        sum_result_squares(nlast, 1)
                    if k == 4:
                        broadcast_half(nlast, 1, FACTOR_BANKS[1], nlast["bc"])
                for k in range(KD - 2):
                    pe.wait_ge(n["lo"], KD + k + 1)
                    for j in range(4):
                        block(j, k, 1)
                for j in range(4):
                    for k in range(KD - 2, KD):
                        if j == 0:
                            pe.wait_ge(n["lo"], KD + k + 1)
                        last = block(j, k, 1)
                    last.then_inc(w_used, 1)

            def project(u0, i, bank):
                pe.wait_ge(w_lo_made, RING * i + (u0 + 1))
                for k in range(KD):
                    last = product(ps[:, bank, :], wblock(u0, k), xtile(k), first=(k == 0), last=(k == KD - 1))
                last.then_inc(w_used, 1)

            def run_ffn(base, f, npre, npost, nlast):
                if base == FFN1:
                    first_group(base, npre, 2)
                    project(base + 2, 0, 2)
                    project(base + 3, 0, 3)
                else:
                    broadcast_half(nlast, 0, FACTOR_BANKS[0], nlast["bc"])
                    first_group_halves(base, npre, nlast)
                sum_squares(npre)
                project(base + 4, 0, 4)
                broadcast_factor(npre, 7)
                project(base + 5, 0, 5)

                def tile(t, i):
                    pe.wait_ge(f["evac"], 2 * i + (t - 1))
                    b = 2 * (t % 2)
                    project(base + 2 * t, i, b)
                    project(base + 2 * t + 1, i, b + 1)

                pe.wait_ge(npre["rsb"], 1)
                project(base + 6, 0, 6)
                project(base + 7, 0, 7)
                with pe.Fori(0, (KF - 4) // 2) as i:
                    tile(4, i)
                    tile(5, i)

                def down_tile(j, i):
                    pe.wait_ge(f["evac"], 2 * i + (KF - 1 + j))
                    for c in range(4):
                        u0 = base + GATE_UP_UNITS + 4 * j + c
                        pe.wait_ge(w_lo_made, 8 * i + (u0 + 1))
                        pe.wait_ge(f["lo"], DOWN_FROM[c] + DOWN_PARTS[c])
                        for k in range(DOWN_PARTS[c]):
                            t = DOWN_FROM[c] + k
                            last = product(ps[:, j, :], wblock(u0, k), htile(t), first=(t == 0), last=(t == KF - 1))
                        last.then_inc(w_used, 1)

                with pe.Fori(0, (KD - 2) // 2) as i:
                    down_tile(0, i)
                    down_tile(1, i)
                down_tile(0, (KD - 2) // 2)
                pe.wait_ge(f["evac"], KF + KD - 2)
                u0 = base + GATE_UP_UNITS + 4 * (KD - 1)
                last_tile(npost, [(u0 + c, 0, DOWN_PARTS[c]) for c in range(4)], htile)

            def gate_half(v, half):
                u0 = MIX + GATES + v
                if half == 0:
                    pe.wait_ge(w_lo_made, u0 + 1)
                    if v:
                        pe.wait_ge(gate_evac, v)
                for k in range(4 * half, 4 * half + 4):
                    last = product(ps[:, 7, :], wblock(u0, k), xtile(k), first=(k == 0), last=(k == KD - 1))
                if half:
                    last.then_inc(w_used, 1)

            def fox_masks(h):
                for b in range(TB):
                    if h:
                        pe.wait_ge(fox["exp"], 4 * (h - 1) + b + 1)
                    nc.tensor.matmul(ps[:, b, b * P:(b + 1) * P], ident_r[:, :], mask_r[:, 1, :],
                                     start=True, stop=False, skip_group_check=True)

            def fox_scores(h, blocks):
                r = DH * (h % 2)
                q, k = T_QA + h // 2, T_KA + h // 2
                for b in blocks:
                    n = (b + 1) * P
                    o = ps[:, b, 0:n]
                    nc.tensor.matmul(o, pick_r[r:r + 40, h:h + 1].to_broadcast([40, P]), cum_r[r:r + 40, 0:n],
                                     start=False, stop=False, skip_group_check=True)
                    product(o, (h_hi[r:r + DH, q, b * P:n], h_lo[r:r + DH, q, b * P:n]),
                            (h_hi[r:r + DH, k, 0:n], h_lo[r:r + DH, k, 0:n]), last=True).then_inc(fox["score"], 1)

            def fox_transpose(h, blocks):
                for b in blocks:
                    pe.wait_ge(fox["norm"], 4 * h + b + 1)
                    if 4 * h + b >= 2:
                        pe.wait_ge(fox["ptl"], 4 * h + b - 1)
                    for j in range(b + 1):
                        last = nc.tensor.transpose(ps[:, 4 + b % 2, j * P:(j + 1) * P], tmp[:, b, j * P:(j + 1) * P],
                                                   ident)
                    last.then_inc(fox["tr"], 1)

            def value_products(steps, done):
                for i, (a, b, t, head, hi, lo) in enumerate(steps):
                    for p in (hi, lo):
                        last = nc.tensor.matmul(ps[:, 6, a:b], v_head(t, head), p, start=(i == 0 and p is hi),
                                                stop=(i + 1 == len(steps) and p is lo), skip_group_check=True)
                last.then_inc(done, 1)

            def fox_values(h):
                pe.wait_ge(fox["ptl"], 4 * (h + 1))
                if h:
                    pe.wait_ge(fox["osum"], h)
                value_products([(j * P, S, j, h, pt_hi[:, j, j * P:S], pt_lo[:, j, j * P:S]) for j in range(TB)],
                               fox["pv"])

            def swa_scores(h):
                r = DH * (h % 2)
                q = T_QB + h // 2
                if h == 0:
                    pe.wait_ge(fox["exp"], 4 * HEADS)
                elif h >= 2:
                    pe.wait_ge(swa["exp"], h - 1)
                def place(b):
                    return ps[:, 2 * (h % 2) + b // 2, 256 * (b % 2):256 * (b % 2) + 256]

                for b in range(TB):
                    if b == 0:
                        nc.tensor.matmul(place(b)[:, 0:P], ident_r[:, :], mask_r[:, 2, :],
                                         start=True, stop=False, skip_group_check=True)
                        nc.tensor.matmul(place(b)[:, P:2 * P], ident_r[:, :], mask_r[:, 1, :],
                                         start=False, stop=False, skip_group_check=True)
                    else:
                        nc.tensor.matmul(place(b), ident_r[:, :], mask_r[:, 0:2, :].rearrange("p a b -> p (a b)"),
                                         start=(b % 2 == 0), stop=False, skip_group_check=True)
                for b in range(TB):
                    k0, k1 = max(0, b - 1) * P, (b + 1) * P
                    last = product(place(b)[:, 2 * P - (k1 - k0):2 * P],
                                   (h_hi[r:r + DH, q, b * P:k1], h_lo[r:r + DH, q, b * P:k1]),
                                   (h_hi[r:r + DH, T_KB, k0:k1], h_lo[r:r + DH, T_KB, k0:k1]), last=True)
                last.then_inc(swa["score"], 1)

            def swa_transpose(h):
                pe.wait_ge(swa["norm"], h + 1)
                if h == 0:
                    pe.wait_ge(fox["ptl"], 4 * HEADS)
                else:
                    pe.wait_ge(swa["ptl"], 2 * h)
                for j in range(TB):
                    o = ps[:, 4 + j // 2, 256 * (j % 2):256 * (j % 2) + 256]
                    last = nc.tensor.transpose(o[:, 0:P], pb[:, h % 2, j, P:2 * P], ident)
                    if j < TB - 1:
                        last = nc.tensor.transpose(o[:, P:2 * P], pb[:, h % 2, j + 1, 0:P], ident)
                    if j % 2:
                        last.then_inc(swa["tr"], 1)

            def swa_values(h):
                pe.wait_ge(swa["ptl"], 2 * (h + 1))
                if h == 0:
                    pe.wait_ge(fox["osum"], HEADS)
                else:
                    pe.wait_ge(swa["osum"], h)
                steps = []
                for j in range(TB):
                    n = min(2 * P, S - j * P)
                    steps.append((j * P, j * P + n, j, HEADS + h % 2, ptb_hi[:, h % 2, 256 * j:256 * j + n],
                                  ptb_lo[:, h % 2, 256 * j:256 * j + n]))
                value_products(steps, swa["pv"])

            def branch_a(d):
                pe.wait_ge(w_lo_made, MIX + BRANCH + d + 1)
                if d == 0:
                    pe.wait_ge(fox["ol"], HEADS)
                for k in range(4):
                    product(ps[:, 2 * (d % 4), :], wblock(MIX + BRANCH + d, k), htile(T_QA + k),
                            first=(k == 0), last=(k == 3))

            def branch_b(d, blocks):
                for k in blocks:
                    last = product(ps[:, 2 * (d % 4) + 1, :], wblock(MIX + BRANCH + d, 4 + k), htile(T_QB + k),
                                   first=(k == 0), last=(k == 3))
                if blocks[-1] == 3:
                    last.then_inc(w_used, 1)

            def run_mixer():
                npre = pre[1]
                first_group_halves(MIX + Q_A, npre, post[0])
                sum_squares(npre)
                project(MIX + K_A, 0, 4)
                broadcast_factor(npre, 7)
                project(MIX + K_A + 1, 0, 5)
                for t in (2, 3):
                    pe.wait_ge(proj_evac, t - 1)
                    project(MIX + K_A + t, 0, t - 2)
                project(MIX + FG, 0, 6)
                for t, (bank, n) in enumerate(((2, 3), (3, 4), (0, 7), (1, 8))):
                    pe.wait_ge(proj_evac, n)
                    project(MIX + Q_B + t, 0, bank)
                project(MIX + K_B, 0, 7)
                pe.wait_ge(proj_evac, 10)
                for u in range(4):
                    pe.wait_ge(w_lo_made, MIX + V_A + u + 1)
                    for kk in range(2):
                        k = 2 * u + kk
                        for t in range(TB):
                            last = product(ps[:, V_BANKS[t], :], xtile(k, t * P, (t + 1) * P),
                                           wblock(MIX + V_A + u, kk, S), first=(k == 0), last=(k == KD - 1))
                    last.then_inc(w_used, 1)
                pe.wait_ge(proj_evac, 11)
                project(MIX + V_B, 0, 3)

                pe.wait_ge(proj_evac, 14)
                gate_half(0, 0)
                gate_half(0, 1)
                pe.wait_ge(proj_evac, 19)
                for t in range(TB):
                    last = nc.tensor.transpose(ps[:, 5, t * P:(t + 1) * P], tmp[:, 0, t * P:(t + 1) * P], ident)
                last.then_inc(swa_v_turned, 1)
                pe.wait_ge(proj_lo, 13)
                pe.wait_ge(fgate, 5)
                pe.wait_ge(consts_split, 1)
                fox_masks(0)
                fox_scores(0, range(TB))
                gate_half(1, 0)
                gate_half(1, 1)
                pe.wait_ge(proj_evac, 20)
                for h in range(HEADS):
                    if h + 1 < HEADS:
                        fox_transpose(h, (0, 1))
                        fox_masks(h + 1)
                        fox_scores(h + 1, (0, 1))
                        fox_transpose(h, (2,))
                        fox_scores(h + 1, (2,))
                        fox_transpose(h, (3,))
                        fox_scores(h + 1, (3,))
                    else:
                        fox_transpose(h, range(TB))
                        swa_scores(0)
                    gate_half(h + 2, 0)
                    fox_values(h)
                    gate_half(h + 2, 1)
                for h in range(HEADS):
                    if h + 1 < HEADS:
                        swa_scores(h + 1)
                    else:
                        branch_a(0)
                    swa_transpose(h)
                    if h < HEADS - 3:
                        gate_half(HEADS + h + 2, 0)
                        swa_values(h)
                        gate_half(HEADS + h + 2, 1)
                    elif h < HEADS - 1:
                        gate_half(2 * HEADS - 1, h - (HEADS - 3))
                        swa_values(h)
                    else:
                        branch_a(1)
                        swa_values(h)

                branch_b(0, range(3))
                branch_b(1, range(3))
                pe.wait_ge(mix_evac, HEADS)
                branch_b(0, (3,))
                branch_b(1, (3,))
                for d in range(2, KD):
                    if d == 3:
                        pe.wait_ge(gate_evac, 2 * KD)
                    if d >= 4:
                        pe.wait_ge(mix_evac, HEADS + d - 3)
                    branch_a(d)
                    branch_b(d, range(4))
                for d in range(KD):
                    pe.wait_ge(mix_evac, HEADS + KD - 1 + d)
                    if d == KD - 1:
                        u0 = MIX + OUT + d
                        last_tile(post[1], [(u0, 0, 3), (u0, 3, KD - 3)], lambda k, a, b: htile(T_MERGED + k, a, b))
                        break
                    pe.wait_ge(w_lo_made, MIX + OUT + d + 1)
                    if d == 0:
                        pe.wait_ge(merged_lo, KD - 1)
                    for k in range(KD):
                        if d == 0 and k == KD - 1:
                            pe.wait_ge(merged_lo, KD)
                        last = product(ps[:, d % 2, :], wblock(MIX + OUT + d, k), htile(T_MERGED + k),
                                       first=(k == 0), last=(k == KD - 1))
                    last.then_inc(w_used, 1)

            pe.wait_ge(fills_made, 1)
            for _ in range(WARM_UP):
                nc.tensor.matmul(ps[:, 7, 0:P], ones[:, :], ones[:, :], start=True, stop=True)
            run_ffn(FFN1, ffn[0], pre[0], post[0], None)
            run_mixer()
            run_ffn(FFN2, ffn[1], pre[2], post[2], post[1])
            n = post[2]
            sum_result_squares(n, 1)
            broadcast_half(n, 1, FACTOR_BANKS[1], n["bc"])
            broadcast_half(n, 1, COPY_BANK, last_factor_out)

        @block.scalar
        def _(act):
            def split_hi(u0, i=0, elems=UNIT):
                s, n = loads_of(u0)
                act.wait_ge(w_loaded[s], 16 * i + n)
                if not (isinstance(i, int) and u0 + RING * i < RING):
                    act.wait_ge(w_used, RING * i + (u0 - RING + 1))
                nc.scalar.activation(w_hi[:, s, 0:elems], raw[:, s, 0:elems], ACT.Copy).then_inc(w_hi_made, 1)

            def copy_factor(n):
                act.wait_ge(n["bc"], 1)
                nc.scalar.activation(rsb[:, :], ps[:, 7, :], ACT.Copy).then_inc(n["rsb"], 1)

            def high_input(k, n, g):
                nc.scalar.activation(xs_hi[:, k, :], x[:, k, :], ACT.Copy, scale=gain[:, g, k:k + 1]).then_inc(n["hi"], 1)

            def square_input(k, n):
                if k >= 2:
                    act.wait_ge(n["acc"], k)
                nc.scalar.activation(sq[:, k % 2, :], x[:, k, :], ACT.Square).then_inc(n["sq"], 1)

            def result_tile(d0, i, bank, n, g, used, evac, unit=None, at=0, elems=UNIT):
                d = i + d0
                act.wait_ge(w_used, used)
                act.wait_ge(n["acc"], d + 1)
                nc.scalar.activation(sq[:, d0 % 2, :], ps[:, bank, :], ACT.Square).then_inc(n["sq"], 1)
                if unit is not None:
                    split_hi(unit, at, elems)
                nc.scalar.activation(y[:, bass.ds(d, 1), :].rearrange("p a b -> p (a b)"), ps[:, bank, :], ACT.Copy,
                                     scale=gain[:, g, bass.ds(d, 1)]).then_inc(evac, 1)

            def last_tile(n, g, used, evac, units, unit, nnext, gnext):
                def squares(h):
                    a, b = h * HALF, (h + 1) * HALF
                    nc.scalar.activation(sq[:, 1, a:b], ps[:, LAST_BANKS[h], a:b], ACT.Square).then_inc(n["sq"], 1)

                def keep(h):
                    a, b = h * HALF, (h + 1) * HALF
                    nc.scalar.activation(y[:, KD - 1, a:b], ps[:, LAST_BANKS[h], a:b], ACT.Copy,
                                         scale=gain[:, g, KD - 1:KD]).then_inc(evac, 1)

                def high(k, h):
                    act.wait_ge(n["x"], h * KD + k + 1)
                    a, b = h * HALF, (h + 1) * HALF
                    nc.scalar.activation(xs_hi[:, k, a:b], x[:, k, a:b], ACT.Copy,
                                         scale=gain[:, gnext, k:k + 1]).then_inc(nnext["hi"], 1)

                act.wait_ge(n["half"], 1)
                act.wait_ge(n["acc"], KD - 1)
                squares(0)
                keep(0)
                for u in units[0:2]:
                    split_hi(u)
                early = 2 if units else 0
                if early:
                    high(0, 0)
                for u in units[2:]:
                    split_hi(u)
                if early:
                    high(1, 0)
                act.wait_ge(w_used, used)
                squares(1)
                if nnext is not None:
                    for k in range(early, 3):
                        high(k, 0)
                    split_hi(unit)
                    high(3, 0)
                keep(1)
                if nnext is not None:
                    for k in range(4, KD):
                        high(k, 0)
                    for k in range(KD):
                        high(k, 1)
                        square_input(k, nnext)

            def run_ffn(base, f, npre, npost, gpost, nnext, gnext, next_base):
                for j in range(4):
                    split_hi(base + 4 + j)
                copy_factor(npre)

                def activate(t, i=0):
                    act.wait_ge(f["scaled"], i + (t + 1))
                    nc.scalar.activation(tmp[:, 0, :], tmp[:, 0, :], ACT.Silu).then_inc(f["silu"], 1)
                    act.wait_ge(f["prod"], i + (t + 1))
                    nc.scalar.activation(h_hi[:, bass.ds(i + t, 1), :].rearrange("p a b -> p (a b)"), tmp[:, 2, :],
                                         ACT.Copy).then_inc(f["hi"], 1)

                activate(0)
                activate(1)

                def tile(t, i):
                    for j in range(2):
                        split_hi(base + 2 * t + 4 + j, i)
                    activate(t, 2 * i)

                with act.Fori(0, (KF - 4) // 2) as i:
                    tile(2, i)
                    tile(3, i)
                for t in (KF - 2, KF - 1):
                    for j in range(2):
                        c = 2 * (t - KF + 2) + j
                        split_hi(base + GATE_UP_UNITS + c, 0, DOWN_PARTS[c] * P)
                    activate(t)

                def down(d0, i, sizes, u0):
                    used = 4 * i + (base + GATE_UP_UNITS + 4 * d0 + 4)
                    for c in range(3):
                        split_hi(u0 + c, i, sizes[c] * P)
                    result_tile(d0, i, d0 % 2, npost, gpost, used, f["evac"], u0 + 3, i, sizes[3] * P)

                u0 = base + GATE_UP_UNITS + 4
                with act.Fori(0, (KD - 2) // 2) as i:
                    down(0, 2 * i, DOWN_PARTS, u0)
                    down(1, 2 * i, DOWN_PARTS, u0 + 4)
                down(KD - 2, 0, DOWN_PARTS, u0 + 4 * (KD - 2))
                last_tile(npost, gpost, base + FFN_UNITS, f["evac"],
                          () if nnext is None else (next_base, next_base + 1, next_base + 2),
                          next_base and next_base + 3, nnext, gnext)

            def high_part(n, dst):
                if n < 8:
                    act.wait_ge(proj_evac, n + 1)
                else:
                    act.wait_ge(proj_val, n - 7)
                nc.scalar.activation(dst, tmp[:, 2 + n % 2, :], ACT.Copy).then_inc(proj_hi, 1)

            def fox_exp(h, blocks):
                for b in blocks:
                    act.wait_ge(fox["max"], 4 * h + b + 1)
                    if h:
                        act.wait_ge(fox["tr"], 4 * (h - 1) + b + 1)
                    n = (b + 1) * P
                    nc.scalar.activation(tmp[:, b, 0:n], ps[:, b, 0:n], ACT.Exp, bias=negmax[:, 0, b:b + 1],
                                         accum_out=rowsum[:, 0, b:b + 1]).then_inc(fox["exp"], 1)

            def swa_exp(h):
                p = h % 2
                act.wait_ge(swa["max"], h + 1)
                nc.scalar.activation(sinkexp[:, p, :], negmax[:, p, :], ACT.Exp, bias=sink[:, h:h + 1])
                if h == 0:
                    act.wait_ge(fox["tr"], 4 * HEADS)
                elif h >= 2:
                    act.wait_ge(swa["tr"], 2 * (h - 1))
                for b in range(TB):
                    last = nc.scalar.activation(pb[:, p, b, :],
                                                ps[:, 2 * p + b // 2, 256 * (b % 2):256 * (b % 2) + 256], ACT.Exp,
                                                bias=negmax[:, p, b:b + 1], accum_out=rowsum[:, p, b:b + 1])
                last.then_inc(swa["exp"], 1)

            def run_mixer():
                for j in range(4):
                    split_hi(MIX + 4 + j)
                copy_factor(pre[1])
                for t in range(4):
                    high_part(t, h_hi[:, T_QA + t, :])
                for t in range(4):
                    split_hi(MIX + K_A + t + 4)
                    high_part(4 + t, h_hi[:, T_KA + t, :])
                split_hi(MIX + FG + 4)
                act.wait_ge(fgate, 3)
                nc.scalar.activation(tmp[0:HEADS, 1, :], tmp[0:HEADS, 1, :], ACT.Exp).then_inc(fgate_act, 1)
                act.wait_ge(fgate_act, 1)
                nc.scalar.activation(tmp[0:HEADS, 1, :], tmp[0:HEADS, 1, :], ACT.Ln, bias=1.0).then_inc(fgate_act, 1)
                act.wait_ge(fgate, 4)
                for r in (0, DH):
                    nc.scalar.activation(cum_r[r:r + HEADS, :], tmp[0:HEADS, 0, :], ACT.Copy,
                                         scale=-1.0).then_inc(fgate_act, 1)
                for t in range(4):
                    split_hi(MIX + Q_B + t + 4)
                    high_part(8 + t, h_hi[:, T_QB + t, :])
                split_hi(MIX + K_B + 4)
                split_hi(MIX + V_A + 4)
                high_part(12, h_hi[:, T_KB, :])
                for u in range(1, 4):
                    split_hi(MIX + V_A + u + 4)
                for t in range(TB):
                    nc.scalar.activation(v_part(t, 0), ps[:, V_BANKS[t], :].rearrange("p (h c) -> p h c", c=DH), ACT.Copy,
                                         scale=rs[:, t:t + 1]).then_inc(v_hi_made, 1)
                split_hi(MIX + V_B + 4)
                split_hi(MIX + GATES + 4)
                act.wait_ge(swa_v_turned, 1)
                for i in range(2):
                    for n in range(2):
                        last = nc.scalar.activation(v_kv_part(i, n, 0), turned(i, n), ACT.Copy)
                last.then_inc(v_hi_made, 1)

                def fox_high(h, blocks):
                    for b in blocks:
                        act.wait_ge(fox["tr"], 4 * h + b + 1)
                        if b == 0 and h:
                            act.wait_ge(fox["pv"], h)
                        nc.scalar.activation(pt_hi[:, 0:b + 1, b * P:(b + 1) * P],
                                             ps[:, 4 + b % 2, 0:(b + 1) * P].rearrange("p (j q) -> p j q", q=P),
                                             ACT.Copy).then_inc(fox["pth"], 1)

                def out_copy(t0, h, n):
                    act.wait_ge(n["pv"], h + 1)
                    nc.scalar.activation(head_sum(t0, h), ps[DH:P, 6, :],
                                         ACT.Copy).then_inc(n["ocopy"], 1)

                def out_high(t0, h, n):
                    act.wait_ge(n["osum"], h + 1)
                    nc.scalar.activation(head_out(h_hi, t0, h), head_sum(t0, h),
                                         ACT.Copy).then_inc(n["oh"], 1)

                fox_exp(0, range(TB))
                for h in range(HEADS):
                    if h + 1 < HEADS:
                        fox_high(h, (0, 1))
                        fox_exp(h + 1, (0, 1))
                        if h:
                            out_high(T_QA, h - 1, fox)
                        fox_high(h, (2, 3))
                        fox_exp(h + 1, (2, 3))
                    else:
                        fox_high(h, range(TB))
                        out_high(T_QA, h - 1, fox)
                        swa_exp(0)
                    split_hi(MIX + GATES + h + 5)
                    out_copy(T_QA, h, fox)
                for h in range(HEADS):
                    for g, n in ((0, 512), (1, 384)):
                        act.wait_ge(swa["tr"], 2 * h + g + 1)
                        if g == 0 and h >= 2:
                            act.wait_ge(swa["pv"], h - 1)
                        if g == 0 and h < 2:
                            act.wait_ge(fox["pv"], HEADS)
                        nc.scalar.activation(ptb_hi[:, h % 2, 512 * g:512 * g + n], ps[:, 4 + g, 0:n],
                                             ACT.Copy).then_inc(swa["pth"], 1)
                    if h:
                        out_high(T_QB, h - 1, swa)
                    else:
                        out_high(T_QA, HEADS - 1, fox)
                    if h + 1 < HEADS:
                        swa_exp(h + 1)
                    if h != HEADS - 2:
                        split_hi(MIX + GATES + HEADS + min(h, HEADS - 2) + 5)
                    out_copy(T_QB, h, swa)
                out_high(T_QB, HEADS - 1, swa)
                act.wait_ge(gate_evac, 2 * KD)
                with act.Fori(0, KD // 4) as i:
                    for j in range(4):
                        at = bass.ds(4 * i + j, 1)
                        for g in (x, gate_b):
                            v = g[:, at, :].rearrange("p a b -> p (a b)")
                            last = nc.scalar.activation(v, v, ACT.Sigmoid)
                        last.then_inc(gate_sig, 1)
                        split_hi(MIX + BRANCH + j + 4, i)
                        act.wait_ge(merged_val, 4 * i + (j + 1))
                        nc.scalar.activation(
                            h_hi[:, bass.ds(4 * i + (T_MERGED + j), 1), :].rearrange("p a b -> p (a b)"),
                            tmp[:, 2, :], ACT.Copy).then_inc(merged_hi, 1)
                for d in range(KD - 1):
                    u0 = MIX + OUT + d
                    result_tile(d, 0, d % 2, post[1], 3, u0 + 1, mix_evac, u0 + 4)
                last_tile(post[1], 3, MIX + MIX_UNITS, mix_evac, (), FFN2 + 3, pre[2], 4)

            act.wait_ge(fills_made, 1)
            nc.scalar.activation(half[:, :], ones[:, 0:TB], ACT.Copy, scale=-0.5).then_inc(half_made, 1)
            act.wait_ge(gain_loaded, 16)
            for j, part in enumerate(X_PARTS):
                act.wait_ge(x_loaded[j], 16)
                for k in part:
                    high_input(k, pre[0], 0)
                if j == 0:
                    split_hi(FFN1)
                    split_hi(FFN1 + 1)
                for k in part:
                    square_input(k, pre[0])
            split_hi(FFN1 + 2)
            split_hi(FFN1 + 3)
            act.wait_ge(small_loaded, 64)
            nc.scalar.activation(ident_r[:, :], cst[:, 0:P], ACT.Copy)
            nc.scalar.activation(pick_r[:, :], cst[:, 4 * P:4 * P + HEADS], ACT.Copy)
            nc.scalar.activation(mask_r[:, :, :], cst[:, P:4 * P].rearrange("p (a b) -> p a b", a=3),
                                 ACT.Copy).then_inc(consts_split, 1)
            run_ffn(FFN1, ffn[0], pre[0], post[0], 1, pre[1], 2, MIX)
            run_mixer()
            run_ffn(FFN2, ffn[1], pre[2], post[2], 5, None, None, None)
            act.wait_ge(last_factor_out, 1)
            nc.scalar.activation(rsb[:, HALF:S], ps[:, COPY_BANK, HALF:S], ACT.Copy).then_inc(last_factor, 1)

        @block.vector
        def _(dve):
            def split_lo(u0, i=0, elems=UNIT):
                s = u0 % RING
                dve.wait_ge(w_hi_made, RING * i + (u0 + 1))
                nc.vector.tensor_tensor(w_lo[:, s, 0:elems], raw[:, s, 0:elems], w_hi[:, s, 0:elems].bitcast(F32),
                                        ALU.subtract).then_inc(w_lo_made, 1)

            def low_input(k, n, g):
                dve.wait_ge(n["hi"], k + 1)
                nc.vector.scalar_tensor_tensor(xs_lo[:, k, :], x[:, k, :], gain[:, g, k:k + 1],
                                               xs_hi[:, k, :].bitcast(F32), ALU.mult, ALU.subtract).then_inc(n["lo"], 1)

            def mean_squares(n, bank, c, t0=0, t1=TB, count=1):
                dve.wait_ge(n["ss"], count)
                nc.vector.tensor_scalar(ms[:, t0:t1], ps[:, bank, t0:t1], c ** -2 / D, c ** -2 * EPS,
                                        ALU.mult, ALU.add).then_inc(n["ms"], 1)

            def diagonal(n, t0=0, t1=TB, count=1):
                dve.wait_ge(n["rs"], count)
                nc.vector.tensor_tensor(tmp[:, 3, t0 * P:t1 * P].rearrange("p (t q) -> p t q", t=t1 - t0),
                                        ident.unsqueeze(1).to_broadcast([P, t1 - t0, P]),
                                        rs[:, t0:t1].unsqueeze(2).to_broadcast([P, t1 - t0, P]),
                                        ALU.mult).then_inc(n["diag"], 1)

            def norm_and_add(n, c, evac, evacs, nnext, g, units, unit):
                def scale(k, h):
                    a, b = h * HALF, (h + 1) * HALF
                    nc.vector.tensor_tensor(y[:, k, a:b], ps[:, FACTOR_BANKS[h], a:b], y[:, k, a:b],
                                            ALU.mult).then_inc(n["t"], 1)

                def add(k, h):
                    a, b = h * HALF, (h + 1) * HALF
                    dve.wait_ge(n["t"], h * KD + k + 1)
                    nc.vector.tensor_tensor(x[:, k, a:b], x[:, k, a:b], y[:, k, a:b], ALU.add).then_inc(n["x"], 1)

                def low(k, h):
                    if nnext is not None:
                        a, b = h * HALF, (h + 1) * HALF
                        dve.wait_ge(nnext["hi"], h * KD + k + 1)
                        nc.vector.scalar_tensor_tensor(xs_lo[:, k, a:b], x[:, k, a:b], gain[:, g, k:k + 1],
                                                       xs_hi[:, k, a:b].bitcast(F32), ALU.mult,
                                                       ALU.subtract).then_inc(nnext["lo"], 1)

                mean_squares(n, SUM_BANKS[0], c, 0, 2)
                diagonal(n, 0, 2)
                for u in units[0:1]:
                    split_lo(u)
                if n is post[1]:
                    dve.wait_ge(x_back, 16 * KD)
                at_squares, at_diagonal = (3, 5) if nnext is not None else (6, 7)
                for h in range(2):
                    tiles = KD if h == 0 or nnext is not None else DVE_TILES
                    dve.wait_ge(evac, evacs + h)
                    dve.wait_ge(n["bc"], h + 1)
                    scale(0, h)
                    for k in range(tiles):
                        if k or h:
                            if k + 1 < tiles:
                                scale(k + 1, h)
                        add(k, h)
                        if h == 0 and k == 0:
                            for u in units[1:2]:
                                split_lo(u)
                            scale(1, h)
                            low(0, h)
                        elif k > (h == 0):
                            low(k - 1, h)
                        if h == 0 and k == at_squares:
                            if unit is not None:
                                dve.wait_ge(w_lo_made, unit)
                                split_lo(unit)
                            mean_squares(n, SUM_BANKS[1], c, 2, TB, 2)
                        if h == 0 and k == at_diagonal:
                            diagonal(n, 2, TB, 2)
                    low(tiles - 1, h)

            def run_ffn(base, f, npre, npost, nnext, gnext, next_base):
                nc.vector.memset(acc_post, 0.0).then_inc(npost["acc"], 1)
                for j in range(4):
                    split_lo(base + 4 + j)
                mean_squares(npre, 6, 1.0)
                diagonal(npre)
                dve.wait_ge(npre["rsb"], 1)

                def evacuate(t, i, bank):
                    dve.wait_ge(w_used, 2 * i + (base + 2 * t + 2))
                    nc.vector.tensor_tensor(tmp[:, 0, :], ps[:, bank, :], rsb[:, :], ALU.mult).then_inc(f["scaled"], 1)
                    nc.vector.tensor_tensor(tmp[:, 1, :], ps[:, bank + 1, :], rsb[:, :], ALU.mult).then_inc(f["evac"], 1)
                    dve.wait_ge(f["silu"], i + (t + 1))
                    dve.wait_ge(f["evac"], i + (t + 1))
                    nc.vector.tensor_tensor(tmp[:, 2, :], tmp[:, 0, :], tmp[:, 1, :], ALU.mult).then_inc(f["prod"], 1)
                    dve.wait_ge(f["hi"], i + (t + 1))
                    nc.vector.tensor_tensor(h_lo[:, bass.ds(i + t, 1), :].rearrange("p a b -> p (a b)"), tmp[:, 2, :],
                                            h_hi[:, bass.ds(i + t, 1), :].rearrange("p a b -> p (a b)").bitcast(F32),
                                            ALU.subtract).then_inc(f["lo"], 1)

                evacuate(0, 0, 0)
                evacuate(1, 0, 2)

                def tile(t, i, bank):
                    for j in range(2):
                        split_lo(base + 2 * t + 4 + j, i)
                    evacuate(t, 2 * i, bank)

                tile(2, 0, 4)
                tile(3, 0, 6)
                with dve.Fori(0, (KF - 6) // 2) as i:
                    tile(4, i, 0)
                    tile(5, i, 2)
                for t in (KF - 2, KF - 1):
                    for j in range(2):
                        c = 2 * (t - KF + 2) + j
                        split_lo(base + GATE_UP_UNITS + c, 0, DOWN_PARTS[c] * P)
                    evacuate(t, 0, 2 * (t % 2))

                def add_tile(d0, i):
                    dve.wait_ge(npost["sq"], i + (d0 + 1))
                    dve.wait_ge(npost["acc"], i + (d0 + 1))
                    nc.vector.tensor_tensor(acc_post, acc_post, sq[:, d0 % 2, :],
                                            ALU.add).then_inc(npost["acc"], 1)

                def down(d0, i, sizes, u0):
                    for c in range(3):
                        split_lo(u0 + c, i, sizes[c] * P)
                    add_tile(d0, i)
                    split_lo(u0 + 3, i, sizes[3] * P)

                u0 = base + GATE_UP_UNITS + 4
                with dve.Fori(0, (KD - 2) // 2) as i:
                    down(0, 2 * i, DOWN_PARTS, u0)
                    down(1, 2 * i, DOWN_PARTS, u0 + 4)
                down(KD - 2, 0, DOWN_PARTS, u0 + 4 * (KD - 2))
                if nnext is not None:
                    norm_and_add(npost, 0.5, f["evac"], KF + KD, nnext, gnext,
                                 (next_base, next_base + 1, next_base + 2), next_base + 3)
                else:
                    norm_and_add(npost, 0.5, f["evac"], KF + KD, None, None, (), None)

            def scaled_tile(n, bank, scale, u):
                dve.wait_ge(w_used, MIX + u + 1)
                nc.vector.scalar_tensor_tensor(tmp[:, 2 + n % 2, :], ps[:, bank, :], scale, rsb[:, :], ALU.mult,
                                               ALU.mult).then_inc(proj_evac, 1)

            def low_part(n, dst_hi, dst_lo):
                dve.wait_ge(proj_hi, n + 1)
                nc.vector.tensor_tensor(dst_lo, tmp[:, 2 + n % 2, :], dst_hi.bitcast(F32), ALU.subtract).then_inc(proj_lo, 1)

            def roped_tile(n, bank, scale, u):
                dve.wait_ge(w_used, MIX + u + 1)
                nc.vector.scalar_tensor_tensor(tmp[:, 0, :], ps[:, bank, :], scale, cos, ALU.mult, ALU.mult)
                for a in range(4):
                    r, o = 32 * a, 32 * (a ^ 1)
                    last = nc.vector.scalar_tensor_tensor(tmp[o:o + 32, 1, :], ps[r:r + 32, bank, :], scale,
                                                          sin[r:r + 32, :], ALU.mult, ALU.mult)
                last.then_inc(proj_evac, 1)
                dve.wait_ge(proj_evac, n + 2)
                nc.vector.tensor_tensor(tmp[:, 2 + n % 2, :], tmp[:, 0, :], tmp[:, 1, :], ALU.add).then_inc(proj_val, 1)

            def fox_max(h, blocks):
                for b in blocks:
                    dve.wait_ge(fox["score"], 4 * h + b + 1)
                    nc.vector.tensor_reduce(negmax[:, 0, b:b + 1], ps[:, b, 0:(b + 1) * P], AX.X, ALU.max,
                                            negate=True).then_inc(fox["max"], 1)

            def fox_recip(h, blocks):
                for b in blocks:
                    dve.wait_ge(fox["exp"], 4 * h + b + 1)
                    nc.vector.reciprocal(recip[:, 0, b:b + 1], rowsum[:, 0, b:b + 1]).then_inc(fox["rec"], 1)

            def swa_max(h):
                p = h % 2
                dve.wait_ge(swa["score"], h + 1)
                nc.vector.tensor_reduce(negmax[:, p, :],
                                        ps[:, 2 * p:2 * p + 2, :].rearrange("p a (b c) -> p (a b) c", b=2),
                                        AX.X, ALU.max, negate=True).then_inc(swa["rawmax"], 1)
                dve.wait_ge(swa["rawmax"], h + 1)
                nc.vector.tensor_scalar(negmax[:, p, :], negmax[:, p, :], nsink[:, h:h + 1], None,
                                        ALU.min).then_inc(swa["max"], 1)

            def swa_recip(h):
                p = h % 2
                dve.wait_ge(swa["exp"], h + 1)
                nc.vector.tensor_tensor(rowsum[:, p, :], rowsum[:, p, :], sinkexp[:, p, :], ALU.add).then_inc(swa["sum"], 1)
                dve.wait_ge(swa["sum"], h + 1)
                nc.vector.reciprocal(recip[:, p, :], rowsum[:, p, :]).then_inc(swa["rec"], 1)

            def run_mixer():
                npre = pre[1]
                for j in range(4):
                    split_lo(MIX + 4 + j)
                mean_squares(npre, 6, 1.0)
                diagonal(npre)
                dve.wait_ge(npre["rsb"], 1)
                for n in range(4):
                    scaled_tile(n, n, SCALE, Q_A + n)
                    low_part(n, h_hi[:, T_QA + n, :], h_lo[:, T_QA + n, :])
                nc.vector.tensor_tensor(cos, cos, rsb[:, :], ALU.mult)
                nc.vector.tensor_tensor(sin, sin, rsb[:, :], ALU.mult).then_inc(rope_scaled, 1)
                for t in range(4):
                    n = 4 + t
                    split_lo(MIX + K_A + t + 4)
                    scaled_tile(n, (4, 5, 0, 1)[t], 1.0, K_A + t)
                    low_part(n, h_hi[:, T_KA + t, :], h_lo[:, T_KA + t, :])
                split_lo(MIX + FG + 4)
                dve.wait_ge(w_used, MIX + FG + 1)
                z, a, zero = tmp[0:HEADS, 0, :], tmp[0:HEADS, 1, :], tmp[0:HEADS, 2, :]
                nc.vector.memset(zero, 0.0)
                nc.vector.tensor_tensor(z, ps[0:HEADS, 6, :], rsb[0:HEADS, :], ALU.mult).then_inc(proj_evac, 1)
                dve.wait_ge(proj_evac, 9)
                nc.vector.tensor_scalar(z, z, fbias[:, 0:1], None, ALU.add).then_inc(fgate, 2)
                dve.wait_ge(fgate, 2)
                nc.vector.scalar_tensor_tensor(a, z, -1.0, z, ALU.mult, ALU.min).then_inc(fgate, 1)
                dve.wait_ge(fgate_act, 2)
                nc.vector.scalar_tensor_tensor(a, z, 0.0, a, ALU.min, ALU.subtract).then_inc(fgate_negative, 1)
                dve.wait_ge(fgate_negative, 1)
                nc.vector.tensor_tensor_scan(z, a, zero, 0.0, ALU.add, ALU.add).then_inc(fgate, 1)
                dve.wait_ge(fgate_act, 4)
                for r in (0, DH):
                    last = nc.vector.scalar_tensor_tensor(cum_r[r + 32:r + 32 + HEADS, :], z, -1.0,
                                                          cum_r[0:HEADS, :].bitcast(F32), ALU.mult, ALU.subtract)
                last.then_inc(fgate, 1)
                dve.wait_ge(rope_scaled, 1)
                dve.wait_ge(fgate, 5)
                for t in range(4):
                    split_lo(MIX + Q_B + t + 4)
                    roped_tile(8 + t, (2, 3, 0, 1)[t], SCALE, Q_B + t)
                    low_part(8 + t, h_hi[:, T_QB + t, :], h_lo[:, T_QB + t, :])
                split_lo(MIX + K_B + 4)
                split_lo(MIX + V_A + 4)
                roped_tile(12, 7, 1.0, K_B)
                low_part(12, h_hi[:, T_KB, :], h_lo[:, T_KB, :])
                for u in range(1, 4):
                    split_lo(MIX + V_A + u + 4)
                for t in range(TB):
                    dve.wait_ge(v_hi_made, t + 1)
                    nc.vector.scalar_tensor_tensor(v_part(t, 1), ps[:, V_BANKS[t], :].rearrange("p (h c) -> p h c", c=DH),
                                                   rs[:, t:t + 1], v_part(t, 0).bitcast(F32), ALU.mult,
                                                   ALU.subtract).then_inc(proj_evac, 1)
                split_lo(MIX + V_B + 4)
                dve.wait_ge(w_used, MIX + V_B + 1)
                nc.vector.tensor_tensor(tmp[:, 0, :], ps[:, 3, :], rsb[:, :], ALU.mult).then_inc(proj_evac, 1)

                def fox_low(h, blocks):
                    for b in blocks:
                        dve.wait_ge(fox["pth"], 4 * h + b + 1)
                        nc.vector.tensor_tensor(pt_lo[:, 0:b + 1, b * P:(b + 1) * P],
                                                ps[:, 4 + b % 2, 0:(b + 1) * P].rearrange("p (j q) -> p j q", q=P),
                                                pt_hi[:, 0:b + 1, b * P:(b + 1) * P].bitcast(F32),
                                                ALU.subtract).then_inc(fox["ptl"], 1)

                def gate_out(v):
                    dve.wait_ge(w_used, MIX + GATES + v + 1)
                    nc.vector.tensor_tensor((x, gate_b)[v % 2][:, v // 2, :], ps[:, 7, :], rsb[:, :],
                                            ALU.mult).then_inc(gate_evac, 1)

                dve.wait_ge(x_saved, 16)
                gate_out(0)
                split_lo(MIX + GATES + 4)
                dve.wait_ge(v_hi_made, TB + 1)
                for i in range(2):
                    for n in range(2):
                        last = nc.vector.tensor_tensor(v_kv_part(i, n, 1), turned(i, n),
                                                       v_kv_part(i, n, 0).bitcast(F32), ALU.subtract)
                last.then_inc(proj_evac, 1)

                def out_sum(t0, h, n):
                    dve.wait_ge(n["ocopy"], h + 1)
                    o = head_sum(t0, h)
                    nc.vector.tensor_tensor(o, ps[0:DH, 6, :], o, ALU.add).then_inc(n["osum"], 1)

                def out_low(t0, h, n, done):
                    dve.wait_ge(n["oh"], h + 1)
                    nc.vector.tensor_tensor(head_out(h_lo, t0, h), head_sum(t0, h), head_out(h_hi, t0, h).bitcast(F32),
                                            ALU.subtract).then_inc(done, 1)

                fox_max(0, range(TB))
                fox_recip(0, range(TB))
                for h in range(HEADS):
                    if h + 1 < HEADS:
                        fox_low(h, (0, 1))
                        fox_max(h + 1, (0, 1))
                        fox_recip(h + 1, (0, 1))
                        gate_out(h + 1)
                        fox_low(h, (2, 3))
                        fox_max(h + 1, (2,))
                        if h:
                            out_low(T_QA, h - 1, fox, fox["ol"])
                        fox_recip(h + 1, (2,))
                        fox_max(h + 1, (3,))
                        fox_recip(h + 1, (3,))
                    else:
                        fox_low(h, (0, 1))
                        gate_out(h + 1)
                        fox_low(h, (2, 3))
                        swa_max(0)
                        out_low(T_QA, h - 1, fox, fox["ol"])
                        swa_recip(0)
                    split_lo(MIX + GATES + h + 5)
                    out_sum(T_QA, h, fox)
                for h in range(HEADS):
                    if h < HEADS - 2:
                        gate_out(HEADS + h + 1)
                    if h + 1 < HEADS:
                        swa_max(h + 1)
                    for g, n in ((0, 512), (1, 384)):
                        dve.wait_ge(swa["pth"], 2 * h + g + 1)
                        nc.vector.tensor_tensor(ptb_lo[:, h % 2, 512 * g:512 * g + n], ps[:, 4 + g, 0:n],
                                                ptb_hi[:, h % 2, 512 * g:512 * g + n].bitcast(F32),
                                                ALU.subtract).then_inc(swa["ptl"], 1)
                    if h:
                        out_low(T_QB, h - 1, swa, mix_evac)
                    else:
                        out_low(T_QA, HEADS - 1, fox, fox["ol"])
                    if h + 1 < HEADS:
                        swa_recip(h + 1)
                    else:
                        dve.wait_ge(mix_evac, h)
                        gate_out(2 * HEADS - 1)
                    if h != HEADS - 2:
                        split_lo(MIX + GATES + HEADS + min(h, HEADS - 2) + 5)
                    out_sum(T_QB, h, swa)
                out_low(T_QB, HEADS - 1, swa, mix_evac)
                dve.wait_ge(mix_evac, HEADS)

                with dve.Fori(0, KD // 4) as i:
                    for j in range(4):
                        b = 2 * j
                        dve.wait_ge(w_used, 4 * i + (MIX + BRANCH + j + 1))
                        dve.wait_ge(gate_sig, 4 * i + (j + 1))
                        at = bass.ds(4 * i + j, 1)
                        nc.vector.tensor_tensor(tmp[:, 0, :], ps[:, b, :], x[:, at, :].rearrange("p a b -> p (a b)"),
                                                ALU.mult)
                        nc.vector.tensor_tensor(tmp[:, 1, :], ps[:, b + 1, :],
                                                gate_b[:, at, :].rearrange("p a b -> p (a b)"),
                                                ALU.mult).then_inc(mix_evac, 1)
                        dve.wait_ge(mix_evac, 4 * i + (HEADS + j + 1))
                        nc.vector.tensor_tensor(tmp[:, 2, :], tmp[:, 0, :], tmp[:, 1, :], ALU.add).then_inc(merged_val, 1)
                        split_lo(MIX + BRANCH + j + 4, i)
                        dve.wait_ge(merged_hi, 4 * i + (j + 1))
                        at = bass.ds(4 * i + (T_MERGED + j), 1)
                        nc.vector.tensor_tensor(h_lo[:, at, :].rearrange("p a b -> p (a b)"), tmp[:, 2, :],
                                                h_hi[:, at, :].rearrange("p a b -> p (a b)").bitcast(F32),
                                                ALU.subtract).then_inc(merged_lo, 1)
                nc.vector.memset(acc_post, 0.0).then_inc(post[1]["acc"], 1)
                for j in range(KD):
                    if j < KD - 1:
                        dve.wait_ge(post[1]["sq"], j + 1)
                        dve.wait_ge(post[1]["acc"], j + 1)
                        nc.vector.tensor_tensor(acc_post, acc_post, sq[:, j % 2, :], ALU.add).then_inc(post[1]["acc"], 1)
                        split_lo(MIX + OUT + j + 4)
                norm_and_add(post[1], 1.0, mix_evac, HEADS + 2 * KD, pre[2], 4, (), FFN2 + 3)

            nc.vector.memset(ones[:, :], 1.0).then_inc(fills_made, 1)
            nc.vector.memset(cum_r[:, :].bitcast(F32), 0.0).then_inc(fills_made, 1)
            for k in range(KD):
                low_input(k, pre[0], 0)
                if k == 0:
                    split_lo(FFN1)
                    split_lo(FFN1 + 1)
            split_lo(FFN1 + 2)
            split_lo(FFN1 + 3)
            dve.wait_ge(small_loaded, 64)
            nc.vector.tensor_scalar(nsink[:, :], sink[:, :], -1.0, None, ALU.mult)
            run_ffn(FFN1, ffn[0], pre[0], post[0], pre[1], 2, MIX)
            run_mixer()
            run_ffn(FFN2, ffn[1], pre[2], post[2], None, None, None)

        @block.gpsimd
        def _(pool):
            def pre_squares(n):
                nc.gpsimd.memset(acc_pre, 0.0).then_inc(n["acc"], 1)
                for k in range(KD):
                    pool.wait_ge(n["sq"], k + 1)
                    pool.wait_ge(n["acc"], k + 1)
                    nc.gpsimd.tensor_tensor(acc_pre, acc_pre, sq[:, k % 2, :], ALU.add).then_inc(n["acc"], 1)

            def result_power(n, h):
                pool.wait_ge(n["ms"], h + 1)
                t = slice(2 * h, 2 * h + 2)
                nc.gpsimd.tensor_tensor(rs[:, t], ms[:, t], half[:, t], ALU.pow).then_inc(n["rs"], 1)

            def last_tiles():
                a, b = HALF, S
                pool.wait_ge(ffn[1]["evac"], KF + KD + 1)
                pool.wait_ge(last_factor, 1)
                for i, k in enumerate(range(DVE_TILES, KD)):
                    nc.gpsimd.tensor_tensor(y[:, k, a:b], rsb[:, a:b], y[:, k, a:b], ALU.mult).then_inc(pool_scaled, 1)
                    pool.wait_ge(pool_scaled, i + 1)
                    nc.gpsimd.tensor_tensor(x[:, k, a:b], x[:, k, a:b], y[:, k, a:b], ALU.add).then_inc(pool_summed, 1)

            def power(n):
                pool.wait_ge(n["ms"], 1)
                nc.gpsimd.tensor_tensor(rs[:, :], ms[:, :], half[:, :], ALU.pow).then_inc(n["rs"], 1)

            pool.wait_ge(half_made, 1)
            pre_squares(pre[0])
            power(pre[0])
            result_power(post[0], 0)
            pool.wait_ge(w_hi_made, MIX + 3)
            pool.wait_ge(w_lo_made, MIX + 2)
            nc.gpsimd.tensor_tensor(w_lo[:, (MIX + 2) % RING, :], raw[:, (MIX + 2) % RING, :],
                                    w_hi[:, (MIX + 2) % RING, :].bitcast(F32), ALU.subtract).then_inc(w_lo_made, 1)
            result_power(post[0], 1)
            pre_squares(pre[1])
            power(pre[1])
            for h in range(HEADS):
                for b in range(TB):
                    pool.wait_ge(fox["rec"], 4 * h + b + 1)
                    n = (b + 1) * P
                    nc.gpsimd.tensor_scalar(tmp[:, b, 0:n], tmp[:, b, 0:n], recip[:, 0, b:b + 1], None,
                                            ALU.mult).then_inc(fox["norm"], 1)
            for h in range(HEADS):
                pool.wait_ge(swa["rec"], h + 1)
                nc.gpsimd.tensor_tensor(pb[:, h % 2], pb[:, h % 2],
                                        recip[:, h % 2, :].unsqueeze(2).to_broadcast([P, TB, 2 * P]),
                                        ALU.mult).then_inc(swa["norm"], 1)
            result_power(post[1], 0)
            result_power(post[1], 1)
            pre_squares(pre[2])
            power(pre[2])
            result_power(post[2], 0)
            result_power(post[2], 1)
            last_tiles()


def tiles(w, rows):
    return w.reshape(rows, P, -1, P).transpose(2, 1, 0, 3).reshape(-1, P, rows * P)


def kernel(**inputs):
    import concourse.bacc as _bacc
    from concourse.bass_utils import run_bass_kernel_spmd as _run

    a = {k: np.asarray(v) for k, v in inputs.items()}

    def gate_up(n):
        g, u = tiles(a[f"ffn{n}_w_gate"][0], KD), tiles(a[f"ffn{n}_w_up"][0], KD)
        return np.ascontiguousarray(np.stack([g, u], axis=1).reshape(-1, P, UNIT))

    w_in = a["w_in"][0]
    fox = HEADS * DH
    cuts = np.cumsum([0, fox, fox, fox, HEADS, fox, P, P, D, D])
    q_a, k_a, v_a, f_a, q_b, k_b, v_b, gate_a, gate_b = (w_in[:, s:e] for s, e in zip(cuts[:-1], cuts[1:]))
    order = np.arange(HEADS).reshape(2, HEADS // 2).T.reshape(-1)
    q_b = q_b.reshape(D, HEADS, DH)[:, order].reshape(D, fox)
    w_swa = a["w_branch_swa"][0].reshape(HEADS, DH, D)[order].reshape(fox, D)
    f_wide = w_in[:, cuts[3]:cuts[3] + P]
    v_units = v_a.reshape(4, 2, P, fox).transpose(0, 2, 1, 3).reshape(4, P, UNIT)
    branch = np.concatenate([tiles(a["w_branch_fox"][0], 4), tiles(w_swa, 4)], axis=2)
    gates = np.stack([tiles(gate_a, KD), tiles(gate_b, KD)], axis=1).reshape(-1, P, UNIT)
    mixw = np.concatenate([tiles(q_a, KD), tiles(k_a, KD), tiles(f_wide, KD), tiles(q_b, KD), tiles(k_b, KD),
                           v_units, tiles(v_b, KD), gates, branch, tiles(a["w_out"][0], KD)], axis=0)

    gains = np.stack([a[n][0].reshape(KD, P).T for n in ("ffn1_pre_g", "ffn1_post_g", "mix_pre_g", "mix_post_g",
                                                         "ffn2_pre_g", "ffn2_post_g")], axis=1)
    sinks = np.broadcast_to(a["swa_sinks"][0][order], (P, HEADS))

    i = np.arange(P)
    before = np.where(i[None, :] > i[:, None], 0.0, MASKED)
    same = np.where(i[None, :] <= i[:, None], 0.0, MASKED)
    pick = ((i[:, None] % 32 == np.arange(HEADS)[None, :]) & (i[:, None] % DH < 40)).astype(np.float32)
    consts = np.concatenate([np.eye(P), before, same, np.full((P, P), MASKED), pick], axis=1).astype(np.float32)
    inv = (np.float32(1.0) / np.float32(10000.0) ** (np.arange(0, DH, 2, dtype=np.float32) / np.float32(DH)))
    ang = (np.arange(S, dtype=np.float32)[:, None] * inv.astype(np.float32)[None, :]).T
    cos, sin = np.cos(ang), np.sin(ang)
    rope = np.stack([np.tile(cos, (4, 1)), np.tile(np.concatenate([sin, -sin]), (2, 1))], axis=1).astype(np.float32)

    arrays = {
        "x_in": a["x"][0].T.reshape(KD, P, S).transpose(1, 0, 2),
        "gu1": gate_up(1), "dn1": tiles(a["ffn1_w_down"][0], KF), "mixw": mixw,
        "gu2": gate_up(2), "dn2": tiles(a["ffn2_w_down"][0], KF), "gains": gains, "sinks": sinks,
        "forget_bias": a["fox_forget_bias"][0].reshape(HEADS, 1), "consts": consts, "rope": rope,
    }
    arrays = {k: np.ascontiguousarray(v) for k, v in arrays.items()}

    nc = _bacc.Bacc("TRN2", target_bir_lowering=False, num_devices=1, dynamic_dma_scratch_size=1024)
    args = [nc.dram_tensor(k, v.shape, F32, kind="ExternalInput").ap() for k, v in arrays.items()]
    x_kept = nc.dram_tensor("x_kept", (P, KD, S), F32).ap()
    out = nc.dram_tensor("out", (P, KD, S), F32, kind="ExternalOutput").ap()
    build(nc, *args, x_kept, out)
    r = _run(nc, [arrays], core_ids=[0])
    got = np.asarray(r.results[0]["out"])
    return np.ascontiguousarray(got.transpose(1, 0, 2).reshape(D, S).T)[None]
```
